# Optimizing a Trainium2 kernel written in Bass

```python
import math
import jax
import jax.numpy as jnp
from jax import lax
import numpy as np

D_MODEL = 1024
BATCH = 1
SEQ = 512
DEPTH = 2

HEAD_DIM = 64
N_HEADS = D_MODEL // HEAD_DIM
MIX_WIDTH = N_HEADS * HEAD_DIM
A_HEADS = N_HEADS // 2
B_HEADS = N_HEADS // 4
B_KV_HEADS = B_HEADS // 2
C_HEADS = N_HEADS // 4
C_KV_HEADS = C_HEADS // 2
DILATED_PATTERNS = ((128, 1), (512, 4), (2048, 16))
C_RADIUS = 128
Q_BLOCK = 128
GRID_W = 64
ROPE_THETA = 10000.0
D_FF = 2816
EPS = 1e-6
MASK_VALUE = -1e30
PROJ_SIZES = (A_HEADS * HEAD_DIM, A_HEADS * HEAD_DIM, A_HEADS * HEAD_DIM,
              B_HEADS * HEAD_DIM, B_KV_HEADS * HEAD_DIM, B_KV_HEADS * HEAD_DIM,
              C_HEADS * HEAD_DIM, C_KV_HEADS * HEAD_DIM, C_KV_HEADS * HEAD_DIM)
PROJ_WIDTH = sum(PROJ_SIZES)

kernel_name = 'hybrid_dilated_axial_window_encoder'

def rms_norm(x, g):
    xf = x.astype(jnp.float32)
    y = xf * lax.rsqrt(jnp.mean(xf * xf, axis=-1, keepdims=True) + EPS)
    return (y * g.astype(jnp.float32)).astype(x.dtype)

def rope_tables(pos, dim):
    inv_freq = 1.0 / (ROPE_THETA ** (jnp.arange(0, dim, 2, dtype=jnp.float32) / dim))
    ang = pos.astype(jnp.float32)[:, None] * inv_freq[None, :]
    ang = jnp.concatenate([ang, ang], axis=-1)
    return jnp.cos(ang), jnp.sin(ang)

def apply_rope(x, cos, sin):
    xf = x.astype(jnp.float32)
    half = xf.shape[-1] // 2
    rot = jnp.concatenate([-xf[..., half:], xf[..., :half]], axis=-1)
    return (xf * cos[:, None, :] + rot * sin[:, None, :]).astype(x.dtype)

def apply_axial_rope(x, cos_r, sin_r, cos_c, sin_c):
    half = x.shape[-1] // 2
    return jnp.concatenate([apply_rope(x[..., :half], cos_r, sin_r),
                            apply_rope(x[..., half:], cos_c, sin_c)], axis=-1)

def to_residue(x, d):
    b, s = x.shape[:2]
    rest = x.shape[2:]
    x = x.reshape((b, s // d, d) + rest)
    return jnp.moveaxis(x, 2, 1).reshape((b * d, s // d) + rest)

def from_residue(x, batch, d):
    n_slots = x.shape[1]
    rest = x.shape[2:]
    x = x.reshape((batch, d, n_slots) + rest)
    return jnp.moveaxis(x, 1, 2).reshape((batch, d * n_slots) + rest)

def banded_attention(q, k, v, radius, sink=None):
    n, seq_len, hq, dh = q.shape
    hkv = k.shape[2]
    rep = hq // hkv
    qb = math.gcd(radius, seq_len)
    nb = seq_len // qb
    kw = qb + 2 * radius
    pad = ((0, 0), (radius, radius), (0, 0), (0, 0))
    kp = jnp.pad(k, pad)
    vp = jnp.pad(v, pad)
    idx = (jnp.arange(nb) * qb)[:, None] + jnp.arange(kw)[None, :]
    kb = kp[:, idx]
    vb = vp[:, idx]
    qr = q.reshape(n, nb, qb, hkv, rep, dh)
    s = jnp.einsum('nbqgrd,nbkgd->nbgrqk', qr, kb,
                   preferred_element_type=jnp.float32) / math.sqrt(dh)
    kpos = idx - radius
    rel = jnp.arange(kw)[None, :] - radius - jnp.arange(qb)[:, None]
    valid = (jnp.abs(rel) <= radius)[None] & ((kpos >= 0) & (kpos < seq_len))[:, None, :]
    s = jnp.where(valid[None, :, None, None], s, MASK_VALUE)
    m = jnp.max(s, axis=-1)
    if sink is not None:
        sink_b = sink.astype(jnp.float32).reshape(hkv, rep)[None, None, :, :, None]
        m = jnp.maximum(m, sink_b)
    p = jnp.exp(s - m[..., None])
    denom = jnp.sum(p, axis=-1)
    if sink is not None:
        denom = denom + jnp.exp(sink_b - m)
    o = jnp.einsum('nbgrqk,nbkgd->nbqgrd', p.astype(v.dtype), vb,
                   preferred_element_type=jnp.float32)
    o = o / jnp.moveaxis(denom, -1, 2)[..., None]
    lse = jnp.moveaxis(m + jnp.log(denom), -1, 2).reshape(n, seq_len, hq)
    return o.reshape(n, seq_len, hq, dh).astype(v.dtype), lse

def dense_gqa_blocked(q, k, v):
    b, s, hq, dh = q.shape
    hkv = k.shape[2]
    rep = hq // hkv
    nb = s // Q_BLOCK
    qs = jnp.moveaxis(q.reshape(b, nb, Q_BLOCK, hkv, rep, dh), 1, 0)
    scale = 1.0 / math.sqrt(dh)

    def one_block(qblk):
        sc = jnp.einsum('bqgrd,bkgd->bgrqk', qblk, k,
                        preferred_element_type=jnp.float32) * scale
        p = jax.nn.softmax(sc, axis=-1)
        return jnp.einsum('bgrqk,bkgd->bqgrd', p.astype(v.dtype), v)

    o = lax.map(one_block, qs)
    return jnp.moveaxis(o, 0, 1).reshape(b, s, hq, dh)

def half_swiglu(x, g, w_gate, w_up, w_down):
    h = rms_norm(x, g)
    u = jax.nn.silu(h @ w_gate) * (h @ w_up)
    return x + 0.5 * (u @ w_down)

def hybrid_mixer(x, g_mix, w_in, a_qn, a_kn, b_qn, b_kn, c_qn, c_kn, c_sink, g_group, w_out,
                 cos1, sin1, cos_r, sin_r, cos_c, sin_c):
    b, s, _ = x.shape
    h = rms_norm(x, g_mix)
    proj = h @ w_in
    offsets = []
    acc = 0
    for size in PROJ_SIZES[:-1]:
        acc += size
        offsets.append(acc)
    aq, ak, av, bq, bk, bv, cq, ck, cv = jnp.split(proj, offsets, axis=-1)

    def heads(t, n_h):
        return t.reshape(b, s, n_h, HEAD_DIM)

    aq = apply_rope(rms_norm(heads(aq, A_HEADS), a_qn), cos1, sin1)
    ak = apply_rope(rms_norm(heads(ak, A_HEADS), a_kn), cos1, sin1)
    av = heads(av, A_HEADS)
    outs, lses = [], []
    for window, dil in DILATED_PATTERNS:
        o, lse = banded_attention(to_residue(aq, dil), to_residue(ak, dil), to_residue(av, dil),
                                  window // (2 * dil))
        outs.append(from_residue(o, b, dil))
        lses.append(from_residue(lse, b, dil))
    mix_w = jax.nn.softmax(jnp.stack(lses, axis=0), axis=0)
    oa = jnp.sum(mix_w[..., None] * jnp.stack(outs, axis=0).astype(jnp.float32),
                 axis=0).astype(x.dtype)

    bq = apply_axial_rope(rms_norm(heads(bq, B_HEADS), b_qn), cos_r, sin_r, cos_c, sin_c)
    bk = apply_axial_rope(rms_norm(heads(bk, B_KV_HEADS), b_kn), cos_r, sin_r, cos_c, sin_c)
    ob = dense_gqa_blocked(bq, bk, heads(bv, B_KV_HEADS))

    cq = apply_rope(rms_norm(heads(cq, C_HEADS), c_qn), cos1, sin1)
    ck = apply_rope(rms_norm(heads(ck, C_KV_HEADS), c_kn), cos1, sin1)
    oc, _ = banded_attention(cq, ck, heads(cv, C_KV_HEADS), C_RADIUS, c_sink)

    wa = A_HEADS * HEAD_DIM
    wb = B_HEADS * HEAD_DIM
    oa = rms_norm(oa.reshape(b, s, wa), g_group[:wa])
    ob = rms_norm(ob.reshape(b, s, wb), g_group[wa:wa + wb])
    oc = rms_norm(oc.reshape(b, s, -1), g_group[wa + wb:])
    return jnp.concatenate([oa, ob, oc], axis=-1) @ w_out

def setup_inputs(seed: int = 0) -> dict:
    key = jax.random.key(seed)
    ks = jax.random.split(key, 20)

    def w(k, shape, fan_in):
        return jax.random.normal(k, shape, jnp.float32) * fan_in ** -0.5

    def gain(k, shape):
        return 1.0 + 0.02 * jax.random.normal(k, shape, jnp.float32)

    return {
        'x': jax.random.normal(ks[0], (BATCH, SEQ, D_MODEL), jnp.float32),
        'ffn1_norm': gain(ks[1], (DEPTH, D_MODEL)),
        'ffn1_w_gate': w(ks[2], (DEPTH, D_MODEL, D_FF), D_MODEL),
        'ffn1_w_up': w(ks[3], (DEPTH, D_MODEL, D_FF), D_MODEL),
        'ffn1_w_down': w(ks[4], (DEPTH, D_FF, D_MODEL), D_FF),
        'mix_norm': gain(ks[5], (DEPTH, D_MODEL)),
        'w_in': w(ks[6], (DEPTH, D_MODEL, PROJ_WIDTH), D_MODEL),
        'a_q_norm': gain(ks[7], (DEPTH, HEAD_DIM)),
        'a_k_norm': gain(ks[8], (DEPTH, HEAD_DIM)),
        'b_q_norm': gain(ks[9], (DEPTH, HEAD_DIM)),
        'b_k_norm': gain(ks[10], (DEPTH, HEAD_DIM)),
        'c_q_norm': gain(ks[11], (DEPTH, HEAD_DIM)),
        'c_k_norm': gain(ks[12], (DEPTH, HEAD_DIM)),
        'c_sink': 0.5 * jax.random.normal(ks[13], (DEPTH, C_HEADS), jnp.float32),
        'group_norm': gain(ks[14], (DEPTH, MIX_WIDTH)),
        'w_out': w(ks[15], (DEPTH, MIX_WIDTH, D_MODEL), MIX_WIDTH),
        'ffn2_norm': gain(ks[16], (DEPTH, D_MODEL)),
        'ffn2_w_gate': w(ks[17], (DEPTH, D_MODEL, D_FF), D_MODEL),
        'ffn2_w_up': w(ks[18], (DEPTH, D_MODEL, D_FF), D_MODEL),
        'ffn2_w_down': w(ks[19], (DEPTH, D_FF, D_MODEL), D_FF),
    }

def reference(x, ffn1_norm, ffn1_w_gate, ffn1_w_up, ffn1_w_down, mix_norm, w_in,
              a_q_norm, a_k_norm, b_q_norm, b_k_norm, c_q_norm, c_k_norm, c_sink,
              group_norm, w_out, ffn2_norm, ffn2_w_gate, ffn2_w_up, ffn2_w_down):
    s = x.shape[1]
    rows = s // GRID_W
    t = jnp.arange(s)
    row = jnp.repeat(jnp.arange(rows), GRID_W)
    col = jnp.tile(jnp.arange(GRID_W), rows)
    cos1, sin1 = rope_tables(t, HEAD_DIM)
    cos_r, sin_r = rope_tables(row, HEAD_DIM // 2)
    cos_c, sin_c = rope_tables(col, HEAD_DIM // 2)
    for l in range(DEPTH):
        x = half_swiglu(x, ffn1_norm[l], ffn1_w_gate[l], ffn1_w_up[l], ffn1_w_down[l])
        x = x + hybrid_mixer(x, mix_norm[l], w_in[l], a_q_norm[l], a_k_norm[l],
                             b_q_norm[l], b_k_norm[l], c_q_norm[l], c_k_norm[l], c_sink[l],
                             group_norm[l], w_out[l],
                             cos1, sin1, cos_r, sin_r, cos_c, sin_c)
        x = half_swiglu(x, ffn2_norm[l], ffn2_w_gate[l], ffn2_w_up[l], ffn2_w_down[l])
    return x


_drawn_inputs = setup_inputs


def setup_inputs(seed=0):
    import zlib

    import numpy as np

    out = dict(_drawn_inputs(seed))
    spreads = {}
    factors = {'ffn1_norm': 4.218,
     'a_q_norm': 5.928,
     'a_k_norm': 5.687,
     'b_q_norm': 7.854,
     'b_k_norm': 7.122,
     'c_q_norm': 8.0,
     'c_k_norm': 8.0,
     'c_sink': 8.0,
     'group_norm': 2.833,
     'ffn2_norm': 8.0}
    for name, (base, spread) in spreads.items():
        noise = np.random.default_rng([zlib.crc32(name.encode()), seed]).standard_normal(out[name].shape)
        drawn = base * np.exp(spread * noise) if base else spread * noise
        out[name] = jnp.asarray(drawn.astype(out[name].dtype))
    for name, factor in factors.items():
        out[name] = (out[name] * factor).astype(out[name].dtype)
    return out
```

```python
import math
from contextlib import ExitStack

import numpy as np

import concourse.bass as bass
from concourse import mybir

ALU = mybir.AluOpType
ACT = mybir.ActivationFunctionType
AX_X = mybir.AxisListType.X
F32 = mybir.dt.float32
F32R = mybir.dt.float32r
BF16 = mybir.dt.bfloat16

P = 128
D_MODEL = 1024
SEQ = 512
DEPTH = 2
HEAD_DIM = 64
HALF = HEAD_DIM // 2
D_FF = 2816
A_HEADS, B_HEADS, C_HEADS = 8, 4, 4
B_KV_HEADS = C_KV_HEADS = 2
GRID_W = 64
C_RADIUS = 128
DILATED_PATTERNS = ((128, 1), (512, 4), (2048, 16))
ROPE_THETA = 10000.0
EPS = 1e-6
MASK_VALUE = -1e30
SCALE = 1.0 / math.sqrt(HEAD_DIM)

TB = SEQ // P
DT = D_MODEL // P
FT = D_FF // P
VW = HEAD_DIM + 1

SLAB = 2048
KW = 512
UP_SLABS = FT
DOWN_SLABS = FT // 2
FFN_SLABS = UP_SLABS + DOWN_SLABS
CHUNKS = 5
PROJ_SLABS = 2 * CHUNKS
OUT_SLABS = 4
LAYER_SLABS = 2 * FFN_SLABS + PROJ_SLABS + OUT_SLABS
PROJ0 = FFN_SLABS
OUT0 = PROJ0 + PROJ_SLABS
FFN_BASE = (0, OUT0 + OUT_SLABS)
N_SLABS = DEPTH * LAYER_SLABS

QK_CHUNKS = 4
TILES = CHUNKS * TB
QK_TILES = QK_CHUNKS * TB
PAIR0 = (8, 11, 0, 4)
PAIRS = (3, 3, 4, 4)
N_PAIRS = 14
V_HEADS = A_HEADS + B_KV_HEADS + C_KV_HEADS
KINDS = 6
UNITS = 64
S_RING = 3
T_LAG, V_LAG = 3, 4
SPLIT_HI_STEPS, SPLIT_LO_STEPS = (8, 10, 12, 14), (16, 18, 20, 22)
SQUARE_B_STEP = 40
GROUPS = ((4, 8 * HEAD_DIM, 4 * HEAD_DIM), (0, 0, 8 * HEAD_DIM), (6, 12 * HEAD_DIM, 4 * HEAD_DIM))
GROUP_TILES = ((4, 5), (0, 1, 2, 3), (6, 7))
RESID_AT = {k: n + 1 for n, k in enumerate((part, d) for part in (1, 2, 3) for d in range(DT)
                                           if d < DT - 1 and (part, d) != (2, 3))}
O_ORDER = (4, 5, 0, 1, 2, 3, 6, 7)

DB = (0, 1, 2, 7, 5, 6, 3, 4)
GATE_BANK, UP_BANK = (0, 1), (2, 7)
SUM_BANK, ROW_BANK = 6, 5
PROJ_BANKS = (0, 1, 2, 7, 5)
SQ_BANK = 6
T_BANK = (3, 4)
S_BANK = (0, 1, 2)
O_BANK = (5, 6)
JUNK_BANK = 7

PACK = {}
_at = 0
for _name, _width in (("ident", P), ("ones", 1), ("nhalf", 8), ("minus", C_HEADS),
                      ("gains", (3 * DEPTH + 1) * DT), ("group_gains", DEPTH * DT), ("sinks", DEPTH * C_HEADS),
                      ("head_gains", DEPTH * KINDS * HEAD_DIM), ("cosA", TB * HALF), ("sinA", TB * HALF),
                      ("nsinA", TB * HALF), ("cosB", TB * HALF), ("sinB", TB * HALF), ("nsinB", TB * HALF)):
    PACK[_name] = (_at, _at + _width)
    _at += _width
PACK_W = _at
TOEP_A = SEQ + (TB - 1) * P
TOEP_C = 3 * P


def c_blocks(qb):
    return range(max(0, qb - 1), min(TB - 1, qb + 1) + 1)


def unit(a):
    return a // 8, (a % 8) // 2, a % 2


def unit_qkv(a):
    i, _, other = unit(a)
    if not other:
        return i // 2, 4 + i // 2, HEAD_DIM * (i % 2), i
    g, pair, v = (i, 8, A_HEADS) if i < B_HEADS else (i - B_HEADS, 11, A_HEADS + B_KV_HEADS)
    return pair + g % 2, pair + 2, HEAD_DIM * (g // 2), v + g // 2


def unit_blocks(a):
    i, qb, other = unit(a)
    return c_blocks(qb) if other and i >= B_HEADS else range(TB)


def transpose_bank_uses():
    count, uses = [0, 0], {}

    def use(key, b):
        count[b] += 1
        uses[key] = (b, count[b])

    for q in range(QK_TILES):
        use(("group", q), q % 2)
    for step in range(UNITS + V_LAG):
        if 0 <= step - T_LAG < UNITS:
            use(("unit", step - T_LAG), (step - T_LAG) % 2)
    for n, j in enumerate(O_ORDER):
        use(("o", j), n % 2)
    assert count[0] == count[1]
    return uses, count[0]


def encoder_trunk(nc, slabs, x_in, small, masks, out):
    uses, T_USES = transpose_bank_uses()
    with ExitStack() as ctx:
        def sb(name, shape, dt=F32, on=ctx):
            return on.enter_context(nc.sbuf_tensor(name, shape, dt))

        def sem(name):
            return ctx.enter_context(nc.semaphore(name))

        x = sb("x", [P, DT, SEQ])
        raw = [sb(f"raw{s}", [P, SLAB]) for s in range(2)]
        w_hi = [sb(f"w_hi{s}", [P, SLAB], F32R) for s in range(2)]
        w_lo = [sb(f"w_lo{s}", [P, SLAB], F32R) for s in range(2)]
        gs = [sb(f"gs{s}", [P, SEQ]) for s in range(2)]
        us = [sb(f"us{s}", [P, SEQ]) for s in range(2)]
        square_sum = us[1]
        pack = sb("pack", [P, PACK_W])
        mask = sb("mask", [P, 2 * TOEP_A + TOEP_C], BF16)
        var_col = sb("var_col", [P, TB])
        rstd_col = sb("rstd_col", [P, TB])
        eps_var = sb("eps_var", [P, TB])
        head_ss = [sb(f"head_ss{s}", [P, 8]) for s in range(2)]
        head_var = [sb(f"head_var{s}", [P, 8]) for s in range(2)]
        head_rstd = [sb(f"head_rstd{s}", [P, 8]) for s in range(2)]
        nsink = sb("nsink", [P, C_HEADS])
        neg_max = sb("neg_max", [P, UNITS])
        table_warm = sb("table_warm", [P, 4])
        sink_exp = sb("sink_exp", [P, C_HEADS, TB])
        den = sb("den", [P, TB])
        rden = [sb(f"rden{s}", [P, TB]) for s in range(2)]
        group_ss = sb("group_ss", [P, 3, TB])
        group_var = sb("group_var", [P, 3, TB])
        group_rstd = sb("group_rstd", [P, 3, TB])
        with ExitStack() as view:
            o_tok = sb("o_tok", [P, TB, D_MODEL], on=view)
            s_masked = [sb(f"s_masked{s}", [P, SEQ], on=view) for s in range(S_RING)]
            probs = [sb(f"probs{s}", [P, SEQ], on=view) for s in range(S_RING)]
            probs_t = [sb(f"probs_t{s}", [P, SEQ], on=view) for s in range(2)]
        h_hi = sb("h_hi", [P, DT, SEQ], F32R)
        h_lo = sb("h_lo", [P, DT, SEQ], F32R)
        with ExitStack() as view:
            u_hi = sb("u_hi", [P, FT, SEQ], F32R, on=view)
            u_lo = sb("u_lo", [P, FT, SEQ], F32R, on=view)
            rstd_row = sb("rstd_row", [P, SEQ], on=view)
        with ExitStack() as view:
            with ExitStack() as early:
                o_hi = sb("o_hi", [P, DT, SEQ], F32R, on=early)
                o_lo = sb("o_lo", [P, DT, SEQ], F32R, on=early)
            qk_hi = sb("qk_hi", [P, N_PAIRS, SEQ], F32R, on=view)
            qk_lo = sb("qk_lo", [P, N_PAIRS, SEQ], F32R, on=view)
            v_tok = sb("v_tok", [P, TB, V_HEADS, VW], on=view)
            rope_cos = sb("rope_cos", [P, KINDS, TB, HEAD_DIM], on=view)
            rope_sin = sb("rope_sin", [P, KINDS, TB, HEAD_DIM], on=view)
            qk_tok = sb("qk_tok", [P, TB, KW], on=view)
        bank = [ctx.enter_context(nc.psum_tensor(f"bank{b}", [P, 512], F32)) for b in range(8)]

        def small_of(name):
            return pack[:, PACK[name][0]:PACK[name][1]]

        ident = small_of("ident")
        ones = small_of("ones")
        nhalf = small_of("nhalf")
        mask_a, count_a = mask[:, 0:TOEP_A], mask[:, TOEP_A:2 * TOEP_A]
        mask_c = mask[:, 2 * TOEP_A:2 * TOEP_A + TOEP_C]

        def column(name, n):
            return pack[:, bass.ds(n + PACK[name][0], 1)]

        small_landed, rope_landed, mask_landed = sem("small_landed"), sem("rope_landed"), sem("mask_landed")
        x_landed = [sem(f"x_landed{i}") for i in range(4)]
        raw_landed = [sem(f"raw_landed{s}") for s in range(2)]
        split_hi, split_lo = sem("split_hi"), sem("split_lo")
        slab_used = sem("slab_used")
        x_ready = sem("x_ready")
        h_hi_ready, h_ready = sem("h_hi_ready"), sem("h_ready")
        sq_ready, sq_added = sem("sq_ready"), sem("sq_added")
        sum_done, var_ready, rstd_ready = sem("sum_done"), sem("var_ready"), sem("rstd_ready")
        row_done, row_ready = sem("row_done"), sem("row_ready")
        gate_done, resid_done = sem("gate_done"), sem("resid_done")
        gate_read, up_read = sem("gate_read"), sem("up_read")
        silu_done, u_ready = sem("silu_done"), sem("u_ready")
        u_hi_ready, u_lo_ready = sem("u_hi_ready"), sem("u_lo_ready")
        eps_var_ready = sem("eps_var_ready")
        tables_ready, v_ones, nsink_ready = sem("tables_ready"), sem("v_ones"), sem("nsink_ready")
        proj_done, tile_squared, rope_parts = sem("proj_done"), sem("tile_squared"), sem("rope_parts")
        heads_summed, rope_sum, roped = sem("heads_summed"), sem("rope_sum"), sem("roped")
        group_done, group_hi = sem("group_done"), sem("group_hi")
        t_read = [sem(f"t_read{b}") for b in range(2)]
        scores_begun = sem("scores_begun")
        s_done, s_read, p_ready, p_used = sem("s_done"), sem("s_read"), sem("p_ready"), sem("p_used")
        pv_done, sink_ready = sem("pv_done"), sem("sink_ready")
        den_ready, rden_ready, o_ready = sem("den_ready"), sem("rden_ready"), sem("o_ready")
        squared, group_var_ready, group_rstd_ready = sem("squared"), sem("group_var_ready"), sem("group_rstd_ready")
        o_scaled, o_turned, o_hi_ready = sem("o_scaled"), sem("o_turned"), sem("o_hi_ready")
        out_stored = sem("out_stored")
        SLOTS = 2
        FREE = 2

        block = ctx.enter_context(nc.Block())

        def slab_end(L, j):
            return LAYER_SLABS * L + j + 1 + SLOTS

        def instance(L, m):
            return 3 * L + m

        @block.sync
        def _(sp):
            early = PACK["head_gains"][0]
            sp.dma_start(pack[:, 0:early], small[:, 0:early]).then_inc(small_landed, 16)
            sp.dma_start(x[:, 0:2, :], x_in[:, 0:2, :]).then_inc(x_landed[0], 16)
            sp.dma_start(raw[0][:, :], slabs[0]).then_inc(raw_landed[0], 16)
            for i in range(1, 4):
                sp.dma_start(x[:, 2 * i:2 * i + 2, :], x_in[:, 2 * i:2 * i + 2, :]).then_inc(x_landed[i], 16)
            sp.dma_start(raw[1][:, :], slabs[1]).then_inc(raw_landed[1], 16)
            sp.dma_start(pack[:, early:], small[:, early:]).then_inc(rope_landed, 16)
            sp.dma_start(mask[:, :], masks).then_inc(mask_landed, 16)
            with sp.Fori(1, N_SLABS // 2) as i:
                for s in range(2):
                    sp.wait_ge(split_lo, 2 * i + (s - 1))
                    sp.dma_start(raw[s][:, :], slabs[bass.ds(2 * i + s, 1)].rearrange("o p c -> p (o c)"))\
                      .then_inc(raw_landed[s], 16)
            sp.wait_ge(split_lo, N_SLABS - 1)
            sp.dma_start(raw[0][:, :], slabs[N_SLABS]).then_inc(raw_landed[0], 16)
            for d in range(DT):
                sp.wait_ge(x_ready, DT * (3 * DEPTH - 1) + d + 1)
                sp.dma_start(out[:, d, :], x[:, d, :]).then_inc(out_stored, 16)
            sp.wait_ge(out_stored, 16 * DT)

        @block.scalar
        def _(act):
            def split(L, j):
                s = j % 2
                act.wait_ge(raw_landed[s], 16 * (LAYER_SLABS // 2) * L + 16 * (j // 2 + 1))
                act.wait_ge(slab_used, LAYER_SLABS * L + j + 1)
                nc.scalar.activation(w_hi[s][:, :], raw[s][:, :], ACT.Copy).then_inc(split_hi, 1)

            def split_step(L, base, s, j):
                act.wait_ge(raw_landed[s], (LAYER_SLABS * 8) * L + 8 * j + (8 * (base - s) + 16))
                act.wait_ge(slab_used, LAYER_SLABS * L + j + (base + 1))
                nc.scalar.activation(w_hi[s][:, :], raw[s][:, :], ACT.Copy).then_inc(split_hi, 1)

            def normal_tile(m, d):
                nc.scalar.activation(h_hi[:, d, :], x[:, d, :], ACT.Copy, scale=column("gains", DT * m + d))\
                  .then_inc(h_hi_ready, 1)
                if d >= 3:
                    act.wait_ge(sq_added, (DT - 1) * m + (d - 2))
                dst = square_sum if d == 0 else gs[d % 2]
                nc.scalar.activation(dst[:, :], x[:, d, :], ACT.Square).then_inc(sq_ready, 1)

            def normal(L, part):
                m = instance(L, part)
                for d in range(DT):
                    act.wait_ge(x_ready, DT * m + (d + 1 - DT))
                    normal_tile(m, d)

            def ffn(L, w):
                base, m = FFN_BASE[w], instance(L, 2 * w)
                f0 = 2 * FT * L + FT * w

                def silu(F, s):
                    act.wait_ge(gate_read, F + (1 + FREE))
                    nc.scalar.activation(gs[s][:, :], gs[s][:, :], ACT.Silu).then_inc(silu_done, 1)

                def hidden_at(i, e):
                    act.wait_ge(u_ready, f0 + 2 * i + (e + 1))
                    nc.scalar.activation(u_hi[:, bass.ds(2 * i + e, 1), :], us[e % 2][:, :].rearrange("p (o c) -> p o c", o=1),
                                         ACT.Copy).then_inc(u_hi_ready, 1)

                split_step(L, base, (base + 1) % 2, 1)
                act.wait_ge(row_done, 2 * L + (w + 1))
                nc.scalar.activation(rstd_row[:, :], bank[ROW_BANK][:, :], ACT.Copy).then_inc(row_ready, 1)
                silu(f0, 0)
                split_step(L, base, base % 2, 2)
                hidden_at(0, 0)
                silu(f0 + 1, 1)
                with act.Fori(1, FT // 2) as i:
                    for e in range(2):
                        split_step(L, base, (base + e + 1) % 2, 2 * i + (e + 1))
                        hidden_at(i - (1 - e), 1 - e)
                        silu(f0 + 2 * i + e, e)
                split_step(L, base, (base + FT + 1) % 2, FT + 1)
                hidden_at(FT // 2 - 1, 1)
                with act.Fori(1, DOWN_SLABS // 2) as i:
                    for e in range(2):
                        split_step(L, base, (base + FT + e) % 2, 2 * i + (FT + e))
                split_step(L, base, (base + FT) % 2, FT + 2 * (DOWN_SLABS // 2))
                split_step(L, base, (base + FT + 1) % 2, FT + DOWN_SLABS)
                normal(L, 2 * w + 1)

            def tile(L, c, tb):
                t = TB * c + tb
                if tb == TB - 1:
                    act.wait_ge(slab_used, slab_end(L, PROJ0 + 2 * c + 1))
                else:
                    act.wait_ge(proj_done, CHUNKS * (TB - 1) * L + (TB - 1) * c + tb + 1)
                X = bank[PROJ_BANKS[t % len(PROJ_BANKS)]]
                if c == QK_CHUNKS:
                    ins = nc.scalar.activation(v_tok[:, tb, 0:A_HEADS, 0:HEAD_DIM],
                                               X[:, :].rearrange("p (h f) -> p h f", f=HEAD_DIM),
                                               ACT.Copy, scale=rstd_col[:, tb:tb + 1])
                else:
                    width = 2 * HEAD_DIM * PAIRS[c]
                    if c < 2:
                        v = A_HEADS + B_KV_HEADS * c
                        nc.scalar.activation(v_tok[:, tb, v:v + 2, 0:HEAD_DIM],
                                             X[:, width:].rearrange("p (h f) -> p h f", f=HEAD_DIM),
                                             ACT.Copy, scale=rstd_col[:, tb:tb + 1])
                    if t:
                        act.wait_ge(heads_summed, QK_TILES * L + t)
                    ins = nc.scalar.activation(bank[SQ_BANK][:, 0:width], X[:, 0:width], ACT.Square)
                ins.then_inc(tile_squared, 1)

            def group(L, q):
                c, tb = q // TB, q % TB
                act.wait_ge(group_done, QK_TILES * L + q + 1)
                nc.scalar.activation(qk_hi[:, PAIR0[c]:PAIR0[c] + PAIRS[c], tb * P:(tb + 1) * P],
                                     bank[T_BANK[q % 2]][:, 0:P * PAIRS[c]].rearrange("p (n t) -> p n t", t=P),
                                     ACT.Copy).then_inc(group_hi, 1)

            def squares(L, n):
                _, c0, width = GROUPS[n]
                for tb in range(TB):
                    k = TB * n + tb
                    if k:
                        act.wait_ge(squared, 3 * TB * L + k)
                    nc.scalar.activation(bank[JUNK_BANK][:, 0:width], o_tok[:, tb, c0:c0 + width], ACT.Square,
                                         accum_out=group_ss[:, n, tb:tb + 1]).then_inc(squared, 1)

            def attention(L):
                for step in range(UNITS + V_LAG):
                    a = step
                    if a < UNITS:
                        i, qb, other = unit(a)
                        width = P * len(unit_blocks(a))
                        act.wait_ge(s_read, UNITS * L + a + 1)
                        if a >= S_RING:
                            act.wait_ge(p_used, UNITS * L + a - S_RING + 1)
                        nc.scalar.activation(probs[a % S_RING][:, 0:width], s_masked[a % S_RING][:, 0:width], ACT.Exp,
                                             bias=neg_max[:, a:a + 1], scale=-1.0).then_inc(p_ready, 1)
                        if other and i >= B_HEADS and qb == TB - 1:
                            g = i - B_HEADS
                            nc.scalar.activation(sink_exp[:, g, :], neg_max[:, 8 * i + 1:8 * i + 8:2], ACT.Exp,
                                                 bias=column("sinks", C_HEADS * L + g)).then_inc(sink_ready, 1)
                    a = step - T_LAG
                    if 0 <= a < UNITS and a % 2:
                        act.wait_ge(p_used, UNITS * L + a + 1)
                        if a >= 2:
                            act.wait_ge(pv_done, UNITS * L + a - 1)
                        width = P * len(unit_blocks(a))
                        nc.scalar.activation(probs_t[1][:, 0:width], bank[T_BANK[1]][:, 0:width], ACT.Copy)\
                          .then_inc(t_read[1], 1)
                    if step in SPLIT_HI_STEPS:
                        j, n = OUT0 + 1, SPLIT_HI_STEPS.index(step)
                        act.wait_ge(raw_landed[j % 2], 8 * LAYER_SLABS * L + 16 * (j // 2 + 1))
                        act.wait_ge(slab_used, LAYER_SLABS * L + j + 1)
                        quarter = slice(n * SLAB // 4, (n + 1) * SLAB // 4)
                        ins = nc.scalar.activation(w_hi[j % 2][:, quarter], raw[j % 2][:, quarter], ACT.Copy)
                        if n == 3:
                            ins.then_inc(split_hi, 1)
                    if step == SQUARE_B_STEP:
                        act.wait_ge(o_ready, 16 * L + 8)
                        squares(L, 0)

            def mixer(L):
                for c in range(CHUNKS):
                    for half in range(2):
                        split(L, PROJ0 + 2 * c + half + 1)
                        if c == 0 and half == 0:
                            act.wait_ge(rstd_ready, instance(L, 1) + 1)
                        if c == CHUNKS - 1 and half == 0:
                            nc.scalar.activation(table_warm[:, 0:1], ones[:, :], ACT.Exp)
                        for tb in range(TB):
                            if half:
                                tile(L, c, tb)
                            elif c:
                                group(L, TB * (c - 1) + tb)
                attention(L)
                for n in (1, 2):
                    act.wait_ge(o_ready, 16 * L + (15 if n == 1 else 16))
                    squares(L, n)
                nc.scalar.activation(table_warm[:, 2:3], ones[:, :], ACT.Silu)
                for n, j in enumerate(O_ORDER):
                    act.wait_ge(o_turned, DT * L + n + 1)
                    nc.scalar.activation(o_hi[:, j, :], bank[T_BANK[n % 2]][:, :], ACT.Copy,
                                         scale=column("group_gains", DT * L + j)).then_inc(o_hi_ready, 1)
                for j in range(2, OUT_SLABS + 1):
                    split(L, OUT0 + j)
                normal(L, 2)

            act.wait_ge(small_landed, 16)
            nc.scalar.activation(table_warm[:, 1:2], ones[:, :], ACT.Silu)
            for d in range(DT):
                act.wait_ge(x_landed[d // 2], 16)
                normal_tile(0, d)
                if d == 1:
                    split(0, 0)
            with act.Fori(0, DEPTH) as L:
                ffn(L, 0)
                mixer(L)
                ffn(L, 1)

        @block.vector
        def _(dve):
            def split_lo_of(s):
                nc.vector.tensor_tensor(w_lo[s][:, :], raw[s][:, :], w_hi[s][:, :].bitcast(F32), ALU.subtract)\
                  .then_inc(split_lo, 1)

            def split(L, j):
                dve.wait_ge(split_hi, LAYER_SLABS * L + j + 1)
                split_lo_of(j % 2)

            def normal_lo(m, d):
                dve.wait_ge(h_hi_ready, DT * m + d + 1)
                nc.vector.scalar_tensor_tensor(h_lo[:, d, :], x[:, d, :], column("gains", DT * m + d),
                                               h_hi[:, d, :].bitcast(F32), ALU.mult, ALU.subtract).then_inc(h_ready, 1)

            def residual(L, part, scale):
                m = instance(L, part)
                for d in range(DT):
                    if (part, d) in RESID_AT:
                        dve.wait_ge(resid_done, len(RESID_AT) * L + RESID_AT[part, d])
                    else:
                        j = {1: FFN_SLABS - 1, 2: OUT0 + (1 if d < 4 else 3), 3: LAYER_SLABS - 1}[part]
                        dve.wait_ge(slab_used, slab_end(L, j))
                    nc.vector.scalar_tensor_tensor(x[:, d, :], bank[DB[d]][:, :], scale, x[:, d, :],
                                                   ALU.mult, ALU.add).then_inc(x_ready, 1)
                    if d:
                        normal_lo(m, d - 1)
                normal_lo(m, DT - 1)

            def token_variance(L, part):
                m = instance(L, part)
                dve.wait_ge(sum_done, m + 1)
                nc.vector.tensor_scalar(var_col[:, :], bank[SUM_BANK][:, 0:TB], 1.0 / D_MODEL, EPS,
                                        ALU.mult, ALU.add).then_inc(var_ready, 1)

            def ffn(L, w):
                base = FFN_BASE[w]
                f0 = 2 * FT * L + FT * w

                def gate(F, s):
                    dve.wait_ge(gate_done, F + 1)
                    nc.vector.tensor_tensor(gs[s][:, :], bank[GATE_BANK[s]][:, :], rstd_row[:, :], ALU.mult)\
                      .then_inc(gate_read, 1)

                def product(j, F, s):
                    dve.wait_ge(slab_used, LAYER_SLABS * L + j + (base + 1 + SLOTS))
                    nc.vector.tensor_tensor(us[s][:, :], bank[UP_BANK[s]][:, :], rstd_row[:, :], ALU.mult)\
                      .then_inc(up_read, 1)
                    dve.wait_ge(silu_done, F + 1)
                    dve.wait_ge(up_read, F + 1)
                    nc.vector.tensor_tensor(us[s][:, :], us[s][:, :], gs[s][:, :], ALU.mult).then_inc(u_ready, 1)

                def split_at(s, j):
                    dve.wait_ge(split_hi, LAYER_SLABS * L + j + (base + 1))
                    split_lo_of(s)

                def hidden_at(i, e):
                    dve.wait_ge(u_hi_ready, f0 + 2 * i + (e + 1))
                    nc.vector.tensor_tensor(u_lo[:, bass.ds(2 * i + e, 1), :],
                                            us[e][:, :].rearrange("p (o c) -> p o c", o=1),
                                            u_hi[:, bass.ds(2 * i + e, 1), :].bitcast(F32),
                                            ALU.subtract).then_inc(u_lo_ready, 1)

                split_at((base + 1) % 2, 1)
                token_variance(L, 2 * w)
                dve.wait_ge(row_ready, 2 * L + (w + 1))
                gate(f0, 0)
                product(0, f0, 0)
                split_at(base % 2, 2)
                hidden_at(0, 0)
                gate(f0 + 1, 1)
                with dve.Fori(1, FT // 2) as i:
                    for e in range(2):
                        product(2 * i + (e - 1), f0 + 2 * i + (e - 1), 1 - e)
                        split_at((base + e + 1) % 2, 2 * i + (e + 1))
                        hidden_at(i - (1 - e), 1 - e)
                        gate(f0 + 2 * i + e, e)
                product(FT - 1, f0 + (FT - 1), 1)
                split_at((base + FT + 1) % 2, FT + 1)
                hidden_at(FT // 2 - 1, 1)
                with dve.Fori(1, DOWN_SLABS // 2) as i:
                    for e in range(2):
                        split_at((base + FT + e) % 2, 2 * i + (FT + e))
                split_at((base + FT) % 2, FT + 2 * (DOWN_SLABS // 2))
                split_at((base + FT + 1) % 2, FT + DOWN_SLABS)
                residual(L, 2 * w + 1, 0.5)

            def tile(L, c, tb):
                t = q = TB * c + tb
                heads = 2 * PAIRS[c]
                width = HEAD_DIM * heads
                X = bank[PROJ_BANKS[t % len(PROJ_BANKS)]]
                s = q % 2
                dve.wait_ge(tile_squared, TILES * L + t + 1)
                if q >= 2:
                    dve.wait_ge(roped, QK_TILES * L + q - 1)
                nc.vector.reduce_sum(head_ss[s][:, 0:heads],
                                     bank[SQ_BANK][:, 0:width].rearrange("p (h f) -> p h f", f=HEAD_DIM),
                                     axis=AX_X).then_inc(heads_summed, 1)
                dve.wait_ge(tables_ready, KINDS * L + (2 * c + 2 if c < 2 else c + 3))
                if q >= TB:
                    dve.wait_ge(group_done, QK_TILES * L + q - TB + 1)
                parts = ((2 * c, 0, 4), (2 * c + 1, 4, 2)) if c < 2 else ((c + 2, 0, heads),)
                axial = c == 0
                for kind, h0, n in parts:
                    cols = slice(h0 * HEAD_DIM, (h0 + n) * HEAD_DIM)
                    cosines = rope_cos[:, kind, tb:tb + 1, :].broadcast_to([P, n, HEAD_DIM])
                    nc.vector.tensor_tensor(qk_tok[:, tb, cols].rearrange("p (h f) -> p h f", f=HEAD_DIM),
                                            X[:, cols].rearrange("p (h f) -> p h f", f=HEAD_DIM), cosines, ALU.mult)
                    for y in range(2):
                        if axial:
                            view, shape = "p (h a y f) -> p y h a f", dict(a=2, y=2, f=HALF // 2)
                            table = rope_sin[:, kind, tb:tb + 1, :].rearrange("p o (a y f) -> p y o a f", **{k: v for k, v in shape.items()})[:, y]\
                                .broadcast_to([P, n, 2, HALF // 2])
                        else:
                            view, shape = "p (h y f) -> p y h f", dict(y=2, f=HALF)
                            table = rope_sin[:, kind, tb:tb + 1, :].rearrange("p o (y f) -> p y o f", y=2)[:, y]\
                                .broadcast_to([P, n, HALF])
                        nc.vector.tensor_tensor(gs[s][:, cols].rearrange(view, **shape)[:, y],
                                                X[:, cols].rearrange(view, **shape)[:, 1 - y], table, ALU.mult)
                dve.wait_ge(heads_summed, QK_TILES * L + q + 1)
                nc.vector.scalar_tensor_tensor(head_var[s][:, 0:heads], head_ss[s][:, 0:heads], 1.0 / HEAD_DIM,
                                               eps_var[:, tb:tb + 1].broadcast_to([P, heads]),
                                               ALU.mult, ALU.add).then_inc(rope_parts, 1)

            def group(L, q):
                c, tb = q // TB, q % TB
                dve.wait_ge(group_hi, QK_TILES * L + q + 1)
                pairs = slice(PAIR0[c], PAIR0[c] + PAIRS[c])
                nc.vector.tensor_tensor(qk_lo[:, pairs, tb * P:(tb + 1) * P],
                                        bank[T_BANK[q % 2]][:, 0:P * PAIRS[c]].rearrange("p (n t) -> p n t", t=P),
                                        qk_hi[:, pairs, tb * P:(tb + 1) * P].bitcast(F32), ALU.subtract)\
                  .then_inc(t_read[q % 2], 1)

            def scores(L, a):
                i, qb, other = unit(a)
                blocks = unit_blocks(a)
                width = P * len(blocks)
                dve.wait_ge(mask_landed, 16)
                dve.wait_ge(s_done, UNITS * L + a + 1)
                if a >= S_RING:
                    dve.wait_ge(p_ready, UNITS * L + a - S_RING + 1)
                nc.vector.sem_inc(scores_begun, 1)
                S = bank[S_BANK[a % S_RING]][:, 0:width]
                dst, low = s_masked[a % S_RING][:, 0:width], neg_max[:, a:a + 1]
                if other and i < B_HEADS:
                    ins = nc.vector.tensor_scalar(dst, S, -SCALE, 3.0e38, ALU.mult, ALU.min, accum_out=low)
                elif other:
                    c0 = P * (blocks[0] - (qb - 1))
                    ins = nc.vector.tensor_tensor_reduce(out=dst, in0=S, in1=mask_c[:, c0:c0 + width], scale=-SCALE,
                                                         scalar=nsink[:, i - B_HEADS:i - B_HEADS + 1],
                                                         op0=ALU.add, op1=ALU.min, accum_out=low)
                else:
                    c0 = P * (TB - 1 - qb)
                    ins = nc.vector.tensor_tensor_reduce(out=dst, in0=S, in1=mask_a[:, c0:c0 + SEQ], scale=-SCALE,
                                                         scalar=3.0e38, op0=ALU.add, op1=ALU.min, accum_out=low)
                ins.then_inc(s_read, 1)

            def finish_head(L, i, other):
                n = 2 * i + other
                O = bank[O_BANK[other]][:, 0:TB * VW].rearrange("p (b f) -> p b f", f=VW)
                dve.wait_ge(pv_done, UNITS * L + 8 * i + 7 + other)
                total = O[:, :, HEAD_DIM]
                if other and i >= B_HEADS:
                    g = i - B_HEADS
                    dve.wait_ge(sink_ready, C_HEADS * L + g + 1)
                    nc.vector.tensor_tensor(den[:, :], total, sink_exp[:, g, :], ALU.add).then_inc(den_ready, 1)
                    dve.wait_ge(den_ready, C_HEADS * L + g + 1)
                    total = den[:, :]
                nc.vector.reciprocal(rden[n % 2][:, :], total).then_inc(rden_ready, 1)
                dve.wait_ge(rden_ready, 16 * L + n + 1)
                c0 = HEAD_DIM * (i if not other else A_HEADS + i)
                nc.vector.tensor_tensor(o_tok[:, :, c0:c0 + HEAD_DIM], O[:, :, 0:HEAD_DIM],
                                        rden[n % 2][:, :].rearrange("p (b o) -> p b o", o=1).broadcast_to([P, TB, HEAD_DIM]),
                                        ALU.mult).then_inc(o_ready, 1)

            def group_variance(L, n):
                dve.wait_ge(squared, 3 * TB * L + TB * (n + 1))
                nc.vector.tensor_scalar(group_var[:, n, :], group_ss[:, n, :], 1.0 / GROUPS[n][2], EPS,
                                        ALU.mult, ALU.add).then_inc(group_var_ready, 1)

            def group_scale(L, n):
                _, c0, width = GROUPS[n]
                dve.wait_ge(group_rstd_ready, 3 * L + n + 1)
                for tb in range(TB):
                    cols = o_tok[:, tb, c0:c0 + width]
                    nc.vector.tensor_scalar(cols, cols, group_rstd[:, n, tb:tb + 1], None, ALU.mult)\
                      .then_inc(o_scaled, 1)

            def attention(L):
                for step in range(UNITS + V_LAG + 1):
                    if step < UNITS:
                        scores(L, step)
                    a = step - T_LAG
                    if 0 <= a < UNITS and a % 2 == 0:
                        dve.wait_ge(p_used, UNITS * L + a + 1)
                        if a >= 2:
                            dve.wait_ge(pv_done, UNITS * L + a - 1)
                        c0 = P * unit(a)[1]
                        nc.vector.tensor_tensor(probs_t[0][:, :], bank[T_BANK[0]][:, :], count_a[:, c0:c0 + SEQ],
                                                ALU.mult).then_inc(t_read[0], 1)
                    if step in SPLIT_LO_STEPS:
                        j, n = OUT0 + 1, SPLIT_LO_STEPS.index(step)
                        dve.wait_ge(split_hi, LAYER_SLABS * L + j + 1)
                        quarter = slice(n * SLAB // 4, (n + 1) * SLAB // 4)
                        ins = nc.vector.tensor_tensor(w_lo[j % 2][:, quarter], raw[j % 2][:, quarter],
                                                      w_hi[j % 2][:, quarter].bitcast(F32), ALU.subtract)
                        if n == 3:
                            ins.then_inc(split_lo, 1)
                    a = step - V_LAG - 1
                    if 0 <= a < UNITS and unit(a)[1] == TB - 1:
                        finish_head(L, unit(a)[0], unit(a)[2])
                    if step == SQUARE_B_STEP + 2:
                        group_variance(L, 0)
                    if step == SQUARE_B_STEP + 6:
                        group_scale(L, 0)

            def mixer(L):
                for c in range(CHUNKS):
                    for half in range(2):
                        split(L, PROJ0 + 2 * c + half + 1)
                        if c == 0 and half == 0:
                            token_variance(L, 1)
                            dve.wait_ge(var_ready, instance(L, 1) + 1)
                            nc.vector.tensor_scalar(eps_var[:, :], var_col[:, :], EPS, None, ALU.mult)\
                              .then_inc(eps_var_ready, 1)
                            dve.wait_ge(eps_var_ready, L + 1)
                        for tb in range(TB):
                            if half and c < QK_CHUNKS:
                                tile(L, c, tb)
                            elif not half and c:
                                group(L, TB * (c - 1) + tb)
                attention(L)
                for n in (1, 2):
                    group_variance(L, n)
                    group_scale(L, n)
                for n, j in enumerate(O_ORDER):
                    dve.wait_ge(o_hi_ready, DT * L + n + 1)
                    nc.vector.scalar_tensor_tensor(o_lo[:, j, :], bank[T_BANK[n % 2]][:, :],
                                                   column("group_gains", DT * L + j), o_hi[:, j, :].bitcast(F32),
                                                   ALU.mult, ALU.subtract).then_inc(t_read[n % 2], 1)
                for j in range(2, OUT_SLABS + 1):
                    split(L, OUT0 + j)
                residual(L, 2, 1.0)

            dve.wait_ge(small_landed, 16)
            for d in range(DT):
                normal_lo(0, d)
                if d == 1:
                    dve.wait_ge(split_hi, 1)
                    split_lo_of(0)
            with dve.Fori(0, DEPTH) as L:
                ffn(L, 0)
                mixer(L)
                ffn(L, 1)

        @block.gpsimd
        def _(pool):
            def sum_squares(m, first):
                for d in range(1, DT):
                    pool.wait_ge(sq_ready, DT * m + d + 1)
                    if d > 1:
                        pool.wait_ge(sq_added, (DT - 1) * m + d - 1)
                    nc.gpsimd.tensor_tensor(square_sum[:, :], square_sum[:, :], gs[d % 2][:, :], ALU.add)\
                      .then_inc(sq_added, 1)

            def token_rstd(m):
                pool.wait_ge(var_ready, m + 1)
                nc.gpsimd.tensor_tensor(rstd_col[:, :], var_col[:, :], nhalf[:, 0:TB], ALU.pow).then_inc(rstd_ready, 1)

            def tables(L, kind):
                axial = kind < 2
                a, f = (2, HALF // 2) if axial else (1, HALF)
                names = ("cosB", "sinB", "nsinB") if axial else ("cosA", "sinA", "nsinA")
                cos, sin, nsin = (small_of(n).rearrange("p (t a f) -> p t a f", t=TB, a=a) for n in names)
                g0 = PACK["head_gains"][0]
                gain = pack[:, bass.ds(KINDS * HEAD_DIM * L + (g0 + kind * HEAD_DIM), HEAD_DIM)]\
                    .rearrange("p (a y f) -> p a y f", a=a, y=2)
                for y in range(2):
                    for dst, wave, src in ((rope_cos, cos, y), (rope_sin, sin if y else nsin, 1 - y)):
                        to = dst[:, kind].rearrange("p t (a y f) -> p t a y f", a=a, y=2)
                        for k in range(a):
                            g = gain[:, k:k + 1, src, :].broadcast_to([P, TB, f])
                            last = nc.gpsimd.tensor_tensor(to[:, :, k, y, :], wave[:, :, k, :], g, ALU.mult)
                last.then_inc(tables_ready, 1)

            def tile(L, q):
                c, tb, s = q // TB, q % TB, q % 2
                heads = 2 * PAIRS[c]
                width = heads * HEAD_DIM
                pool.wait_ge(rope_parts, QK_TILES * L + q + 1)
                nc.gpsimd.tensor_tensor(head_rstd[s][:, 0:heads], head_var[s][:, 0:heads], nhalf[:, 0:heads], ALU.pow)
                part = qk_tok[:, tb, 0:width]
                nc.gpsimd.tensor_tensor(part, part, gs[s][:, 0:width], ALU.add).then_inc(rope_sum, 1)
                pool.wait_ge(rope_sum, QK_TILES * L + q + 1)
                part = part.rearrange("p (h f) -> p h f", f=HEAD_DIM)
                factor = head_rstd[s][:, 0:heads].rearrange("p (h o) -> p h o", o=1).broadcast_to([P, heads, HEAD_DIM])
                nc.gpsimd.tensor_tensor(part, part, factor, ALU.mult).then_inc(roped, 1)

            def mixer(L):
                pool.wait_ge(rope_landed, 16)
                pool.wait_ge(slab_used, slab_end(L, FFN_SLABS - 1))
                s0 = PACK["sinks"][0]
                nc.gpsimd.tensor_tensor(nsink[:, :], pack[:, bass.ds(C_HEADS * L + s0, C_HEADS)], small_of("minus"), ALU.mult)\
                  .then_inc(nsink_ready, 1)
                nc.gpsimd.memset(v_tok[:, :, :, HEAD_DIM:VW], 1.0).then_inc(v_ones, 1)
                tables(L, 0)
                token_rstd(instance(L, 1))
                for kind in range(1, KINDS):
                    tables(L, kind)
                for q in range(QK_TILES):
                    tile(L, q)
                for n in range(3):
                    pool.wait_ge(group_var_ready, 3 * L + n + 1)
                    nc.gpsimd.tensor_tensor(group_rstd[:, n, :], group_var[:, n, :], nhalf[:, 0:TB], ALU.pow)\
                      .then_inc(group_rstd_ready, 1)

            pool.wait_ge(small_landed, 16)
            sum_squares(0, True)
            with pool.Fori(0, DEPTH) as L:
                token_rstd(instance(L, 0))
                sum_squares(instance(L, 1), False)
                mixer(L)
                sum_squares(instance(L, 2), False)
                token_rstd(instance(L, 2))
                sum_squares(instance(L, 3), False)

        @block.tensor
        def _(pe):
            def three(dst, a_hi, a_lo, b_hi, b_lo, start, stop):
                nc.tensor.matmul(dst, a_hi, b_hi, start=start, stop=False)
                nc.tensor.matmul(dst, a_hi, b_lo, start=False, stop=False)
                return nc.tensor.matmul(dst, a_lo, b_hi, start=False, stop=stop)

            def sum_of_squares(L, part):
                m = instance(L, part)
                pe.wait_ge(sq_added, (DT - 1) * m + (DT - 1))
                for tb in range(TB):
                    last = nc.tensor.matmul(bank[SUM_BANK][:, tb:tb + 1], square_sum[:, tb * P:(tb + 1) * P],
                                            ones[:, :], start=True, stop=True)
                last.then_inc(sum_done, 1)

            def rstd_as_row(L, w):
                pe.wait_ge(rstd_ready, instance(L, 2 * w) + 1)
                for tb in range(TB):
                    last = nc.tensor.matmul(bank[ROW_BANK][:, tb * P:(tb + 1) * P],
                                            rstd_col[:, tb:tb + 1].broadcast_to([P, P]), ident, start=True, stop=True)
                last.then_inc(row_done, 1)

            def ffn(L, w):
                base, m = FFN_BASE[w], instance(L, 2 * w)
                f0 = 2 * FT * L + FT * w

                def gemm(dst, s, c0, h_first):
                    for k in range(DT):
                        if h_first:
                            pe.wait_ge(h_ready, DT * m + k + 1)
                        cols = slice(c0 + k * P, c0 + (k + 1) * P)
                        last = three(dst[:, :], w_hi[s][:, cols], w_lo[s][:, cols], h_hi[:, k, :], h_lo[:, k, :],
                                     k == 0, k == DT - 1)
                    return last

                def up_slab(s, e, j, F, first=None):
                    pe.wait_ge(split_lo, LAYER_SLABS * L + j + (base + 1))
                    pe.wait_ge(gate_read, F + (FREE - 1))
                    gemm(bank[GATE_BANK[e]], s, 0, first == 0).then_inc(gate_done, 1)
                    if first == 0:
                        sum_of_squares(L, 2 * w)
                    if first == 1:
                        rstd_as_row(L, w)
                    if first is None:
                        pe.wait_ge(up_read, F - 1)
                    gemm(bank[UP_BANK[e]], s, DT * P, False).then_inc(slab_used, 1)

                def down_slab(s, j, i, e0, first=False, last=False):
                    pe.wait_ge(split_lo, LAYER_SLABS * L + j + (base + 1))

                    def part(d, e, start, stop):
                        f = bass.ds(2 * i + (2 * e0 + e), 1)
                        cols = slice(e * D_MODEL + d * P, e * D_MODEL + (d + 1) * P)
                        return three(bank[DB[d]][:, :], w_hi[s][:, cols], w_lo[s][:, cols], u_hi[:, f, :], u_lo[:, f, :],
                                     start, stop)

                    if last:
                        pe.wait_ge(u_lo_ready, f0 + FT)
                        for d in range(DT):
                            part(d, 0, False, False)
                            part(d, 1, False, True).then_inc(resid_done if d < DT - 1 else slab_used, 1)
                        return
                    for e in range(2):
                        pe.wait_ge(u_lo_ready, f0 + 2 * i + (2 * e0 + e + 1))
                        for d in (4, 5, 6, 7, 0, 1, 2, 3):
                            if first and e == 0 and d == 0:
                                pe.wait_ge(gate_read, f0 + (FT + FREE))
                                pe.wait_ge(up_read, f0 + FT)
                            ins = part(d, e, first and e == 0, False)
                    ins.then_inc(slab_used, 1)

                up_slab(base % 2, 0, 0, f0, first=0)
                up_slab((base + 1) % 2, 1, 1, f0 + 1, first=1)
                with pe.Fori(1, FT // 2) as i:
                    for e in range(2):
                        up_slab((base + e) % 2, e, 2 * i + e, f0 + 2 * i + e)
                down_slab((base + FT) % 2, FT, 0, 0, first=True)
                with pe.Fori(0, DOWN_SLABS // 2 - 1) as i:
                    down_slab((base + FT + 1) % 2, 2 * i + (FT + 1), 2 * i, 1)
                    down_slab((base + FT) % 2, 2 * i + (FT + 2), 2 * i, 2)
                down_slab((base + FT + 1) % 2, FT + DOWN_SLABS - 2, 0, DOWN_SLABS - 2)
                down_slab((base + FT) % 2, FT + DOWN_SLABS - 1, 0, DOWN_SLABS - 1, last=True)

            def wait_bank(L, key):
                b, n = uses[key]
                if n > 1:
                    pe.wait_ge(t_read[b], T_USES * L + n - 1)
                return bank[T_BANK[b]]

            def wait_copied(L, key):
                b, n = uses[key]
                pe.wait_ge(t_read[b], T_USES * L + n)

            def group(L, q):
                c, tb = q // TB, q % TB
                pe.wait_ge(roped, QK_TILES * L + q + 1)
                dst = wait_bank(L, ("group", q))
                for n in range(PAIRS[c]):
                    last = nc.tensor.transpose(dst[:, n * P:(n + 1) * P], qk_tok[:, tb, n * P:(n + 1) * P], ident)
                last.then_inc(group_done, 1)

            def projection(L):
                m = instance(L, 1)
                for c in range(CHUNKS):
                    for half in range(2):
                        j = PROJ0 + 2 * c + half
                        pe.wait_ge(split_lo, LAYER_SLABS * L + j + 1)
                        for tb in range(TB):
                            t = TB * c + tb
                            if not half:
                                if c:
                                    group(L, TB * (c - 1) + tb)
                                past = t - len(PROJ_BANKS)
                                if past >= 0:
                                    pe.wait_ge(rope_parts, QK_TILES * L + past + 1)
                            for k in range(4):
                                kk = 4 * half + k
                                if c == 0 and tb == 0:
                                    pe.wait_ge(h_ready, DT * m + kk + 1)
                                rows = slice(tb * P, (tb + 1) * P)
                                last = three(bank[PROJ_BANKS[t % len(PROJ_BANKS)]][:, :], h_hi[:, kk, rows], h_lo[:, kk, rows],
                                             w_hi[j % 2][:, k * KW:(k + 1) * KW], w_lo[j % 2][:, k * KW:(k + 1) * KW],
                                             kk == 0, kk == DT - 1)
                            if tb == TB - 1:
                                last.then_inc(slab_used, 1)
                            elif half:
                                last.then_inc(proj_done, 1)
                        if c == 0 and half == 0:
                            sum_of_squares(L, 1)

            def scores(L, a):
                i, qb, other = unit(a)
                if a >= S_RING:
                    pe.wait_ge(s_read, UNITS * L + a - S_RING + 1)
                elif a:
                    pe.wait_ge(tile_squared, TILES * L + QK_TILES + a)
                else:
                    for q in (QK_TILES - 2, QK_TILES - 1):
                        wait_copied(L, ("group", q))
                pq, pk, r, _ = unit_qkv(a)
                rows = slice(r, r + HEAD_DIM)
                blocks = unit_blocks(a)
                keys = slice(P * blocks[0], P * (blocks[-1] + 1))
                queries = slice(P * qb, P * (qb + 1))
                three(bank[S_BANK[a % S_RING]][:, 0:P * len(blocks)], qk_hi[rows, pq, queries], qk_lo[rows, pq, queries],
                      qk_hi[rows, pk, keys], qk_lo[rows, pk, keys], True, True).then_inc(s_done, 1)

            def turn(L, a):
                other = unit(a)[2]
                pe.wait_ge(p_ready, UNITS * L + a + 1)
                dst = wait_bank(L, ("unit", a))
                n = len(unit_blocks(a))
                for b in range(n):
                    at = b if other else n - 1 - b
                    last = nc.tensor.transpose(dst[:, at * P:(at + 1) * P], probs[a % S_RING][:, b * P:(b + 1) * P], ident)
                last.then_inc(p_used, 1)

            def values(L, a):
                i, qb, other = unit(a)
                v = unit_qkv(a)[3]
                wait_copied(L, ("unit", a))
                if qb == 0 and i == 0:
                    pe.wait_ge(rope_parts, QK_TILES * (L + 1))
                    pe.wait_ge(tile_squared, TILES * (L + 1))
                    pe.wait_ge(v_ones, L + 1)
                elif qb == 0:
                    pe.wait_ge(o_ready, 16 * L + 2 * i - 1 + other)
                blocks = unit_blocks(a)
                for n, kb in enumerate(blocks):
                    at = n if other else len(blocks) - 1 - n
                    last = nc.tensor.matmul(bank[O_BANK[other]][:, qb * VW:(qb + 1) * VW],
                                            probs_t[other][:, at * P:(at + 1) * P], v_tok[:, kb, v, :],
                                            start=n == 0, stop=n == len(blocks) - 1)
                last.then_inc(pv_done, 1)

            def attention(L):
                for step in range(UNITS + V_LAG):
                    if step < UNITS:
                        scores(L, step)
                    if 0 <= step - T_LAG < UNITS:
                        turn(L, step - T_LAG)
                    if 0 <= step - V_LAG:
                        values(L, step - V_LAG)

            def output(L):
                n = 0
                for g, tiles in enumerate(GROUP_TILES):
                    pe.wait_ge(o_scaled, 3 * TB * L + TB * (g + 1))
                    for j in tiles:
                        dst = wait_bank(L, ("o", j))
                        for tb in range(TB):
                            last = nc.tensor.transpose(dst[:, tb * P:(tb + 1) * P], o_tok[:, tb, j * P:(j + 1) * P], ident)
                        last.then_inc(o_turned, 1)
                for dh in range(2):
                    for kh in range(2):
                        j = OUT0 + 2 * dh + kh
                        pe.wait_ge(split_lo, LAYER_SLABS * L + j + 1)
                        if dh == 0 and kh == 0:
                            wait_copied(L, ("o", 2))
                            wait_copied(L, ("o", 3))
                            pe.wait_ge(s_read, UNITS * (L + 1))
                            pe.wait_ge(squared, 3 * TB * (L + 1))
                        if dh == 0 and kh == 1:
                            wait_copied(L, ("o", 6))
                            wait_copied(L, ("o", 7))
                        for dd in range(4):
                            for k in range(4):
                                cols = slice(k * KW + dd * P, k * KW + (dd + 1) * P)
                                last = three(bank[DB[4 * dh + dd]][:, :], w_hi[j % 2][:, cols], w_lo[j % 2][:, cols],
                                             o_hi[:, 4 * kh + k, :], o_lo[:, 4 * kh + k, :],
                                             kh == 0 and k == 0, kh == 1 and k == 3)
                            if dd == 3:
                                last.then_inc(slab_used, 1)
                            elif kh:
                                last.then_inc(resid_done, 1)

            nc.tensor.sem_inc(slab_used, SLOTS)
            nc.tensor.sem_inc(gate_read, FREE)
            pe.wait_ge(small_landed, 16)
            with pe.Fori(0, DEPTH) as L:
                ffn(L, 0)
                projection(L)
                attention(L)
                output(L)
                ffn(L, 1)


def _rope_tables(pos, dim):
    inv_freq = (1.0 / (np.float32(ROPE_THETA) ** (np.arange(0, dim, 2, dtype=np.float32) / np.float32(dim)))).astype(np.float32)
    ang = (pos.astype(np.float32)[:, None] * inv_freq[None, :]).astype(np.float32)
    return np.cos(ang.astype(np.float64)).astype(np.float32), np.sin(ang.astype(np.float64)).astype(np.float32)


def _constants():
    t = np.arange(SEQ)
    cos_a, sin_a = _rope_tables(t, HEAD_DIM)
    cos_r, sin_r = _rope_tables(t // GRID_W, HALF)
    cos_c, sin_c = _rope_tables(t % GRID_W, HALF)
    cos_b, sin_b = np.concatenate([cos_r, cos_c], 1), np.concatenate([sin_r, sin_c], 1)

    def by_block(a):
        return a.reshape(TB, P, -1).transpose(1, 0, 2).reshape(P, -1)

    cols = {"ident": np.eye(P), "ones": np.ones((P, 1)), "nhalf": np.full((P, 8), -0.5), "minus": np.full((P, C_HEADS), -1.0),
            "cosA": by_block(cos_a), "sinA": by_block(sin_a), "nsinA": by_block(-sin_a),
            "cosB": by_block(cos_b), "sinB": by_block(sin_b), "nsinB": by_block(-sin_b)}
    rel = np.arange(TOEP_A)[None, :] - (TB - 1) * P - np.arange(P)[:, None]
    count = sum(((rel % dil == 0) & (np.abs(rel) <= (window // (2 * dil)) * dil)).astype(np.float32)
                for window, dil in DILATED_PATTERNS)
    rel_c = np.arange(TOEP_C)[None, :] - P - np.arange(P)[:, None]
    masks = np.concatenate([np.where(count > 0, 0.0, MASK_VALUE), count,
                            np.where(np.abs(rel_c) <= C_RADIUS, 0.0, MASK_VALUE)], 1)
    return {k: v.astype(np.float32) for k, v in cols.items()}, masks


def _slabs(a):
    out = np.empty((N_SLABS + 1, P, SLAB), np.float32)
    q_order = [0, 2, 1, 3]
    cols, at = [], 0
    for heads in (A_HEADS, A_HEADS, A_HEADS, B_HEADS, B_KV_HEADS, B_KV_HEADS, C_HEADS, C_KV_HEADS, C_KV_HEADS):
        c = np.arange(at, at + heads * HEAD_DIM).reshape(heads, HEAD_DIM)
        cols.append((c[q_order] if heads == 4 else c).ravel())
        at += heads * HEAD_DIM
    cols = np.concatenate(cols[3:] + cols[:3])
    n = 0
    for l in range(DEPTH):
        for w in (1, 2):
            if w == 2:
                w_in = a["w_in"][l][:, cols].reshape(2, 4, P, CHUNKS, KW)
                out[n:n + PROJ_SLABS] = w_in.transpose(3, 0, 2, 1, 4).reshape(PROJ_SLABS, P, SLAB)
                n += PROJ_SLABS
                w_out = a["w_out"][l].reshape(2, 4, P, 2, KW)
                out[n:n + OUT_SLABS] = w_out.transpose(3, 0, 2, 1, 4).reshape(OUT_SLABS, P, SLAB)
                n += OUT_SLABS
            both = np.stack([a[f"ffn{w}_w_gate"][l], a[f"ffn{w}_w_up"][l]])
            both = both.reshape(2, DT, P, FT, P)
            out[n:n + FT] = both.transpose(3, 2, 0, 1, 4).reshape(FT, P, SLAB)
            n += FT
            down = a[f"ffn{w}_w_down"][l].reshape(DOWN_SLABS, 2, P, D_MODEL)
            out[n:n + DOWN_SLABS] = down.transpose(0, 2, 1, 3).reshape(DOWN_SLABS, P, SLAB)
            n += DOWN_SLABS
    assert n == N_SLABS
    out[n] = out[0]
    return out


def kernel(**inputs):
    import concourse.bacc as _bacc
    import ml_dtypes as _ml
    from concourse.bass_utils import run_bass_kernel_spmd as _run

    a = {k: np.asarray(v) for k, v in inputs.items()}
    cols, masks = _constants()

    def by_tile(g):
        return g.reshape(-1, DT, P).transpose(2, 0, 1).reshape(P, -1)

    norms = np.stack([a[n][l] for l in range(DEPTH) for n in ("ffn1_norm", "mix_norm", "ffn2_norm")] + [a["ffn1_norm"][0]])
    heads = np.stack([a[n][l] for l in range(DEPTH) for n in
                      ("b_q_norm", "b_k_norm", "c_q_norm", "c_k_norm", "a_q_norm", "a_k_norm")])
    cols["gains"] = by_tile(norms)
    cols["group_gains"] = by_tile(a["group_norm"])
    cols["head_gains"] = np.broadcast_to(heads.reshape(1, -1), (P, heads.size))
    cols["sinks"] = np.broadcast_to(a["c_sink"].reshape(1, -1), (P, a["c_sink"].size))
    arrays = {
        "slabs": _slabs(a),
        "x_in": np.ascontiguousarray(a["x"][0].T.reshape(DT, P, SEQ).transpose(1, 0, 2)),
        "small": np.ascontiguousarray(np.concatenate([cols[k] for k in PACK], 1).astype(np.float32)),
        "masks": masks.astype(_ml.bfloat16),
    }
    nc = _bacc.Bacc("TRN2", target_bir_lowering=False, num_devices=1)
    args = [nc.dram_tensor(k, v.shape, mybir.dt.from_np(v.dtype), kind="ExternalInput").ap() for k, v in arrays.items()]
    out = nc.dram_tensor("out", (P, DT, SEQ), F32, kind="ExternalOutput").ap()
    encoder_trunk(nc, *args, out)
    r = _run(nc, [arrays], core_ids=[0])
    y = r.results[0]["out"]
    return y.transpose(1, 0, 2).reshape(D_MODEL, SEQ).T.reshape(1, SEQ, D_MODEL)
```

```python
import math
from contextlib import ExitStack

import numpy as np

import concourse.bass as bass
from concourse import mybir

ALU = mybir.AluOpType
ACT = mybir.ActivationFunctionType
AX_X = mybir.AxisListType.X
F32 = mybir.dt.float32
F32R = mybir.dt.float32r
BF16 = mybir.dt.bfloat16

P = 128
D_MODEL = 1024
SEQ = 512
DEPTH = 2
HEAD_DIM = 64
HALF = HEAD_DIM // 2
D_FF = 2816
A_HEADS, B_HEADS, C_HEADS = 8, 4, 4
B_KV_HEADS = C_KV_HEADS = 2
GRID_W = 64
C_RADIUS = 128
DILATED_PATTERNS = ((128, 1), (512, 4), (2048, 16))
ROPE_THETA = 10000.0
EPS = 1e-6
MASK_VALUE = -1e30
SCALE = 1.0 / math.sqrt(HEAD_DIM)

TB = SEQ // P
DT = D_MODEL // P
FT = D_FF // P
VW = HEAD_DIM + 1

SLAB = 2048
KW = 512
UP_SLABS = FT
DOWN_SLABS = FT // 2
FFN_SLABS = UP_SLABS + DOWN_SLABS
CHUNKS = 5
PROJ_SLABS = 2 * CHUNKS
OUT_SLABS = 4
LAYER_SLABS = 2 * FFN_SLABS + PROJ_SLABS + OUT_SLABS
PROJ0 = FFN_SLABS
OUT0 = PROJ0 + PROJ_SLABS
FFN_BASE = (0, OUT0 + OUT_SLABS)
N_SLABS = DEPTH * LAYER_SLABS

QK_CHUNKS = 4
TILES = CHUNKS * TB
QK_TILES = QK_CHUNKS * TB
PAIR0 = (8, 11, 0, 4)
PAIRS = (3, 3, 4, 4)
N_PAIRS = 14
V_HEADS = A_HEADS + B_KV_HEADS + C_KV_HEADS
KINDS = 6
TABLES_AFTER = {0: 2, 1: 3, 4: 4, 5: 5}
UNITS = 64
S_RING = 3
T_LAG, V_LAG = 3, 5
SPLIT_HI_STEPS, SPLIT_LO_STEPS = (8, 10, 12, 14), (16, 18, 20, 22)
GROUPS = ((8 * HEAD_DIM, 4 * HEAD_DIM, (2, 2)), (0, 8 * HEAD_DIM, (6, 2)), (12 * HEAD_DIM, 4 * HEAD_DIM, (2, 2)))
SQUARES = [(n, part, tb) for n, part in ((0, 0), (0, 1), (1, 0), (1, 1), (2, 0), (2, 1)) for tb in range(TB)]
SQUARE_STEPS = (28, 31, 34, 37, 44, 45, 46, 47, 49, 51, 53, 55, 61, 61, 62, 62)
VARIANCE_STEPS = {49: 0, 63: 1}
SCALE_STEPS = {51: (0, (0,)), 52: (0, (1,)), 53: (0, (2,)), 54: (0, (3,)), 64: (1, tuple(range(TB)))}
GROUP_AT = ((0, 1), (0, 2), (1, 0), (1, 1))
RESID_AT = {k: n + 1 for n, k in enumerate((part, d) for part in (1, 2, 3) for d in range(DT)
                                           if d < DT - 1 and (part, d) != (2, 3))}

DB = (0, 1, 2, 7, 5, 6, 3, 4)
GATE_BANK, UP_BANK = (0, 2), (1, 7)
SUM_BANK, ROW_BANK = 6, 5
PROJ_BANKS = (0, 1, 2, 7, 5)
SQ_BANK = 6
T_BANK = (3, 4, 5)
O_T_BANK = (0, 1, 2, 0, 1, 2, 0, 1)
S_BANK = (0, 1, 2)
O_BANK = (5, 6)
JUNK_BANK = 7

PACK = {}
_at = 0
for _name, _width in (("ident", P), ("ones", 1), ("nhalf", 8), ("minus", C_HEADS),
                      ("gains", (3 * DEPTH + 1) * DT), ("group_gains", DEPTH * DT), ("sinks", DEPTH * C_HEADS),
                      ("head_gains", DEPTH * KINDS * HEAD_DIM), ("cosA", TB * HALF), ("sinA", TB * HALF),
                      ("nsinA", TB * HALF), ("cosB", TB * HALF), ("sinB", TB * HALF), ("nsinB", TB * HALF)):
    PACK[_name] = (_at, _at + _width)
    _at += _width
PACK_W = _at
TOEP_A = SEQ + (TB - 1) * P
TOEP_C = 3 * P


def c_blocks(qb):
    return range(max(0, qb - 1), min(TB - 1, qb + 1) + 1)


def unit_order():
    units = [(i, qb, 0) for i in range(2) for qb in range(TB)]
    for i in range(6):
        for qb in range(TB):
            units += [(i, qb, 1), (i + 2, qb, 0)]
    return units + [(i, qb, 1) for i in (6, 7) for qb in range(TB)]


UNIT_ORDER = unit_order()
HEADS_ENDING = [(i, other) for i, qb, other in UNIT_ORDER if qb == TB - 1]


def unit(a):
    return UNIT_ORDER[a]


def head_number(i, other):
    return HEADS_ENDING.index((i, other))


def head_units(i, other):
    at = [a for a in range(UNITS) if unit(a)[0] == i and unit(a)[2] == other]
    return slice(at[0], at[-1] + 1, at[1] - at[0])


GROUP_HEADS = ((head_number(1, 1) + 1, head_number(3, 1) + 1), (head_number(5, 0) + 1, head_number(7, 0) + 1),
               (head_number(5, 1) + 1, head_number(7, 1) + 1))


def unit_qkv(a):
    i, _, other = unit(a)
    if not other:
        return i // 2, 4 + i // 2, HEAD_DIM * (i % 2), i
    g, pair, v = (i, 8, A_HEADS) if i < B_HEADS else (i - B_HEADS, 11, A_HEADS + B_KV_HEADS)
    return pair + g % 2, pair + 2, HEAD_DIM * (g // 2), v + g // 2


def unit_blocks(a):
    i, qb, other = unit(a)
    return c_blocks(qb) if other and i >= B_HEADS else range(TB)


def transpose_bank_uses():
    count, uses = [0, 0, 0], {}

    def use(key, b):
        count[b] += 1
        uses[key] = (b, count[b])

    for q in range(QK_TILES):
        use(("group", q), q % 2)
    for step in range(UNITS + V_LAG):
        if 0 <= step - T_LAG < UNITS:
            use(("unit", step - T_LAG), (step - T_LAG) % 2)
    for j in range(DT):
        use(("o", j), O_T_BANK[j])
    return uses, count


def encoder_trunk(nc, slabs, x_in, small, masks, out):
    uses, T_USES = transpose_bank_uses()
    with ExitStack() as ctx:
        def sb(name, shape, dt=F32, on=ctx):
            return on.enter_context(nc.sbuf_tensor(name, shape, dt))

        def sem(name):
            return ctx.enter_context(nc.semaphore(name))

        x = sb("x", [P, DT, SEQ])
        raw = [sb(f"raw{s}", [P, SLAB]) for s in range(2)]
        w_hi = [sb(f"w_hi{s}", [P, SLAB], F32R) for s in range(2)]
        w_lo = [sb(f"w_lo{s}", [P, SLAB], F32R) for s in range(2)]
        gs = [sb(f"gs{s}", [P, SEQ]) for s in range(2)]
        us = [sb(f"us{s}", [P, SEQ]) for s in range(2)]
        square_sum = us[1]
        pack = sb("pack", [P, PACK_W])
        mask = sb("mask", [P, 2 * TOEP_A + TOEP_C], BF16)
        var_col = sb("var_col", [P, TB])
        rstd_col = sb("rstd_col", [P, TB])
        eps_var = sb("eps_var", [P, TB])
        head_ss = [sb(f"head_ss{s}", [P, 8]) for s in range(2)]
        head_var = [sb(f"head_var{s}", [P, 8]) for s in range(2)]
        head_rstd = [sb(f"head_rstd{s}", [P, 8]) for s in range(2)]
        nsink = sb("nsink", [P, C_HEADS])
        neg_max = sb("neg_max", [P, UNITS])
        table_warm = sb("table_warm", [P, 4])
        sink_exp = sb("sink_exp", [P, C_HEADS, TB])
        den = sb("den", [P, TB])
        rden = [sb(f"rden{s}", [P, TB]) for s in range(2)]
        group_ss = sb("group_ss", [P, 3, 2, TB])
        group_var = sb("group_var", [P, 3, TB])
        group_rstd = sb("group_rstd", [P, 3, TB])
        with ExitStack() as view:
            o_tok = sb("o_tok", [P, TB, D_MODEL], on=view)
            s_masked = [sb(f"s_masked{s}", [P, SEQ], on=view) for s in range(S_RING)]
            probs = [sb(f"probs{s}", [P, SEQ], on=view) for s in range(S_RING)]
            probs_t = [sb(f"probs_t{s}", [P, SEQ], on=view) for s in range(2)]
        h_hi = sb("h_hi", [P, DT, SEQ], F32R)
        h_lo = sb("h_lo", [P, DT, SEQ], F32R)
        with ExitStack() as view:
            u_hi = sb("u_hi", [P, FT, SEQ], F32R, on=view)
            u_lo = sb("u_lo", [P, FT, SEQ], F32R, on=view)
            rstd_row = sb("rstd_row", [P, SEQ], on=view)
        with ExitStack() as view:
            qk_hi = sb("qk_hi", [P, N_PAIRS, SEQ], F32R, on=view)
            qk_lo = sb("qk_lo", [P, N_PAIRS, SEQ], F32R, on=view)
            v_tok = sb("v_tok", [P, TB, V_HEADS, VW], on=view)
            rope_cos = sb("rope_cos", [P, KINDS, TB, HEAD_DIM], on=view)
            rope_sin = sb("rope_sin", [P, KINDS, TB, HEAD_DIM], on=view)
            qk_tok = sb("qk_tok", [P, TB, KW], on=view)
        o_hi, o_lo = qk_hi, qk_lo
        bank = [ctx.enter_context(nc.psum_tensor(f"bank{b}", [P, 512], F32)) for b in range(8)]

        def small_of(name):
            return pack[:, PACK[name][0]:PACK[name][1]]

        ident = small_of("ident")
        ones = small_of("ones")
        nhalf = small_of("nhalf")
        mask_a, count_a = mask[:, 0:TOEP_A], mask[:, TOEP_A:2 * TOEP_A]
        mask_c = mask[:, 2 * TOEP_A:2 * TOEP_A + TOEP_C]

        def column(name, n):
            return pack[:, bass.ds(n + PACK[name][0], 1)]

        small_landed, rope_landed, mask_landed = sem("small_landed"), sem("rope_landed"), sem("mask_landed")
        x_landed = [sem(f"x_landed{i}") for i in range(4)]
        raw_landed = [sem(f"raw_landed{s}") for s in range(2)]
        half_landed, half_hi = sem("half_landed"), sem("half_hi")
        split_hi, split_lo = sem("split_hi"), sem("split_lo")
        slab_used = sem("slab_used")
        x_ready = sem("x_ready")
        h_hi_ready, h_ready = sem("h_hi_ready"), sem("h_ready")
        sq_ready, sq_added = sem("sq_ready"), sem("sq_added")
        sum_done, var_ready, rstd_ready = sem("sum_done"), sem("var_ready"), sem("rstd_ready")
        row_done, row_ready = sem("row_done"), sem("row_ready")
        gate_done, resid_done = sem("gate_done"), sem("resid_done")
        gate_read, up_read = sem("gate_read"), sem("up_read")
        silu_done, u_ready = sem("silu_done"), sem("u_ready")
        u_hi_ready, u_lo_ready = sem("u_hi_ready"), sem("u_lo_ready")
        eps_var_ready = sem("eps_var_ready")
        tables_ready, v_ones, nsink_ready = sem("tables_ready"), sem("v_ones"), sem("nsink_ready")
        proj_done, tile_squared, rope_parts = sem("proj_done"), sem("tile_squared"), sem("rope_parts")
        head_var_ready = sem("head_var_ready")
        heads_summed, rope_sum, roped = sem("heads_summed"), sem("rope_sum"), sem("roped")
        group_done, group_hi = sem("group_done"), sem("group_hi")
        t_read = [sem(f"t_read{b}") for b in range(3)]
        scores_begun = sem("scores_begun")
        s_done, s_read, p_ready, p_used = sem("s_done"), sem("s_read"), sem("p_ready"), sem("p_used")
        pv_done, sink_ready = sem("pv_done"), sem("sink_ready")
        den_ready, rden_ready, o_ready = sem("den_ready"), sem("rden_ready"), sem("o_ready")
        squared, group_var_ready, group_rstd_ready = sem("squared"), sem("group_var_ready"), sem("group_rstd_ready")
        o_scaled, o_turned, o_hi_ready = sem("o_scaled"), sem("o_turned"), sem("o_hi_ready")
        out_stored = sem("out_stored")
        SLOTS = 2
        FREE = 2

        block = ctx.enter_context(nc.Block())

        def slab_end(L, j):
            return LAYER_SLABS * L + j + 1 + SLOTS

        def instance(L, m):
            return 3 * L + m

        @block.sync
        def _(sp):
            early = PACK["head_gains"][0]
            sp.dma_start(pack[:, 0:early], small[:, 0:early]).then_inc(small_landed, 16)
            sp.dma_start(x[:, 0:2, :], x_in[:, 0:2, :]).then_inc(x_landed[0], 16)
            half = SLAB // 2
            sp.dma_start(raw[0][:, 0:half], slabs[0, :, 0:half]).then_inc(half_landed, 16)
            sp.dma_start(raw[0][:, half:], slabs[0, :, half:]).then_inc(raw_landed[0], 16)
            for i in range(1, 4):
                sp.dma_start(x[:, 2 * i:2 * i + 2, :], x_in[:, 2 * i:2 * i + 2, :]).then_inc(x_landed[i], 16)
            sp.dma_start(raw[1][:, :], slabs[1]).then_inc(raw_landed[1], 16)
            sp.dma_start(pack[:, early:], small[:, early:]).then_inc(rope_landed, 16)
            sp.dma_start(mask[:, :], masks).then_inc(mask_landed, 16)
            with sp.Fori(1, N_SLABS // 2) as i:
                for s in range(2):
                    sp.wait_ge(split_lo, 2 * i + (s - 1))
                    sp.dma_start(raw[s][:, :], slabs[bass.ds(2 * i + s, 1)].rearrange("o p c -> p (o c)"))\
                      .then_inc(raw_landed[s], 16)
            sp.wait_ge(split_lo, N_SLABS - 1)
            sp.dma_start(raw[0][:, :], slabs[N_SLABS]).then_inc(raw_landed[0], 16)
            for d in range(DT):
                sp.wait_ge(x_ready, DT * (3 * DEPTH - 1) + d + 1)
                sp.dma_start(out[:, d, :], x[:, d, :]).then_inc(out_stored, 16)
            sp.wait_ge(out_stored, 16 * DT)

        @block.scalar
        def _(act):
            def split(L, j):
                s = j % 2
                act.wait_ge(raw_landed[s], 16 * (LAYER_SLABS // 2) * L + 16 * (j // 2 + 1))
                act.wait_ge(slab_used, LAYER_SLABS * L + j + 1)
                nc.scalar.activation(w_hi[s][:, :], raw[s][:, :], ACT.Copy).then_inc(split_hi, 1)

            def split_step(L, base, s, j):
                act.wait_ge(raw_landed[s], (LAYER_SLABS * 8) * L + 8 * j + (8 * (base - s) + 16))
                act.wait_ge(slab_used, LAYER_SLABS * L + j + (base + 1))
                nc.scalar.activation(w_hi[s][:, :], raw[s][:, :], ACT.Copy).then_inc(split_hi, 1)

            def normal_tile(m, d):
                nc.scalar.activation(h_hi[:, d, :], x[:, d, :], ACT.Copy, scale=column("gains", DT * m + d))\
                  .then_inc(h_hi_ready, 1)
                if d >= 3:
                    act.wait_ge(sq_added, (DT - 1) * m + (d - 2))
                dst = square_sum if d == 0 else gs[d % 2]
                nc.scalar.activation(dst[:, :], x[:, d, :], ACT.Square).then_inc(sq_ready, 1)

            def normal(L, part):
                m = instance(L, part)
                for d in range(DT):
                    act.wait_ge(x_ready, DT * m + (d + 1 - DT))
                    normal_tile(m, d)

            def ffn(L, w):
                base, m = FFN_BASE[w], instance(L, 2 * w)
                f0 = 2 * FT * L + FT * w

                def silu(F, s):
                    act.wait_ge(gate_read, F + (1 + FREE))
                    nc.scalar.activation(gs[s][:, :], gs[s][:, :], ACT.Silu).then_inc(silu_done, 1)

                def hidden_at(i, e):
                    act.wait_ge(u_ready, f0 + 2 * i + (e + 1))
                    nc.scalar.activation(u_hi[:, bass.ds(2 * i + e, 1), :], us[e % 2][:, :].rearrange("p (o c) -> p o c", o=1),
                                         ACT.Copy).then_inc(u_hi_ready, 1)

                split_step(L, base, (base + 1) % 2, 1)
                split_step(L, base, base % 2, 2)
                act.wait_ge(row_done, 2 * L + (w + 1))
                nc.scalar.activation(rstd_row[:, :], bank[ROW_BANK][:, :], ACT.Copy).then_inc(row_ready, 1)
                silu(f0, 0)
                hidden_at(0, 0)
                silu(f0 + 1, 1)
                with act.Fori(1, FT // 2) as i:
                    for e in range(2):
                        split_step(L, base, (base + e + 1) % 2, 2 * i + (e + 1))
                        hidden_at(i - (1 - e), 1 - e)
                        silu(f0 + 2 * i + e, e)
                split_step(L, base, (base + FT + 1) % 2, FT + 1)
                hidden_at(FT // 2 - 1, 1)
                with act.Fori(1, DOWN_SLABS // 2) as i:
                    for e in range(2):
                        split_step(L, base, (base + FT + e) % 2, 2 * i + (FT + e))
                split_step(L, base, (base + FT) % 2, FT + 2 * (DOWN_SLABS // 2))
                split_step(L, base, (base + FT + 1) % 2, FT + DOWN_SLABS)
                normal(L, 2 * w + 1)

            def tile(L, c, tb):
                t = TB * c + tb
                if tb == TB - 1:
                    act.wait_ge(slab_used, slab_end(L, PROJ0 + 2 * c + 1))
                else:
                    act.wait_ge(proj_done, CHUNKS * (TB - 1) * L + (TB - 1) * c + tb + 1)
                X = bank[PROJ_BANKS[t % len(PROJ_BANKS)]]
                if c == QK_CHUNKS:
                    ins = nc.scalar.activation(v_tok[:, tb, 0:A_HEADS, 0:HEAD_DIM],
                                               X[:, :].rearrange("p (h f) -> p h f", f=HEAD_DIM),
                                               ACT.Copy, scale=rstd_col[:, tb:tb + 1])
                else:
                    width = 2 * HEAD_DIM * PAIRS[c]
                    if c < 2:
                        v = A_HEADS + B_KV_HEADS * c
                        nc.scalar.activation(v_tok[:, tb, v:v + 2, 0:HEAD_DIM],
                                             X[:, width:].rearrange("p (h f) -> p h f", f=HEAD_DIM),
                                             ACT.Copy, scale=rstd_col[:, tb:tb + 1])
                    if t:
                        act.wait_ge(heads_summed, QK_TILES * L + t)
                    ins = nc.scalar.activation(bank[SQ_BANK][:, 0:width], X[:, 0:width], ACT.Square)
                ins.then_inc(tile_squared, 1)

            def group(L, q):
                c, tb = q // TB, q % TB
                act.wait_ge(group_done, QK_TILES * L + q + 1)
                nc.scalar.activation(qk_hi[:, PAIR0[c]:PAIR0[c] + PAIRS[c], tb * P:(tb + 1) * P],
                                     bank[T_BANK[q % 2]][:, 0:P * PAIRS[c]].rearrange("p (n t) -> p n t", t=P),
                                     ACT.Copy).then_inc(group_hi, 1)

            def squares(L, k):
                n, part, tb = SQUARES[k]
                c0, _, heads = GROUPS[n]
                c0, width = c0 + HEAD_DIM * heads[0] * part, HEAD_DIM * heads[part]
                if tb == 0:
                    act.wait_ge(o_ready, 16 * L + GROUP_HEADS[n][part])
                if k:
                    act.wait_ge(squared, len(SQUARES) * L + k)
                nc.scalar.activation(bank[JUNK_BANK][:, 0:width], o_tok[:, tb, c0:c0 + width], ACT.Square,
                                     accum_out=group_ss[:, n, part, tb:tb + 1]).then_inc(squared, 1)

            def attention(L):
                for step in range(UNITS + V_LAG):
                    a = step
                    if a < UNITS:
                        i, qb, other = unit(a)
                        width = P * len(unit_blocks(a))
                        act.wait_ge(s_read, UNITS * L + a + 1)
                        if a >= S_RING:
                            act.wait_ge(p_used, UNITS * L + a - S_RING + 1)
                        nc.scalar.activation(probs[a % S_RING][:, 0:width], s_masked[a % S_RING][:, 0:width], ACT.Exp,
                                             bias=neg_max[:, a:a + 1], scale=-1.0).then_inc(p_ready, 1)
                        if other and i >= B_HEADS and qb == TB - 1:
                            g = i - B_HEADS
                            nc.scalar.activation(sink_exp[:, g, :], neg_max[:, head_units(i, other)], ACT.Exp,
                                                 bias=column("sinks", C_HEADS * L + g)).then_inc(sink_ready, 1)
                    a = step - T_LAG
                    if 0 <= a < UNITS and unit(a)[2]:
                        act.wait_ge(p_used, UNITS * L + a + 1)
                        if a >= 2:
                            act.wait_ge(pv_done, UNITS * L + a - 1)
                        width = P * len(unit_blocks(a))
                        nc.scalar.activation(probs_t[a % 2][:, 0:width], bank[T_BANK[a % 2]][:, 0:width], ACT.Copy)\
                          .then_inc(t_read[a % 2], 1)
                    if step in SPLIT_HI_STEPS:
                        j, n = OUT0 + 1, SPLIT_HI_STEPS.index(step)
                        act.wait_ge(raw_landed[j % 2], 8 * LAYER_SLABS * L + 16 * (j // 2 + 1))
                        act.wait_ge(slab_used, LAYER_SLABS * L + j + 1)
                        quarter = slice(n * SLAB // 4, (n + 1) * SLAB // 4)
                        ins = nc.scalar.activation(w_hi[j % 2][:, quarter], raw[j % 2][:, quarter], ACT.Copy)
                        if n == 3:
                            ins.then_inc(split_hi, 1)
                    for k, at in enumerate(SQUARE_STEPS):
                        if at == step:
                            squares(L, k)

            def mixer(L):
                for c in range(CHUNKS):
                    for half in range(2):
                        split(L, PROJ0 + 2 * c + half + 1)
                        if c == 0 and half == 0:
                            act.wait_ge(rstd_ready, instance(L, 1) + 1)
                        if c == CHUNKS - 1 and half == 0:
                            nc.scalar.activation(table_warm[:, 0:1], ones[:, :], ACT.Exp)
                        for tb in range(TB):
                            if c and (half, tb) in GROUP_AT:
                                group(L, TB * (c - 1) + GROUP_AT.index((half, tb)))
                            if half:
                                tile(L, c, tb)
                attention(L)
                for j in range(DT):
                    if j == TB:
                        for k in range(len(SQUARE_STEPS), len(SQUARES)):
                            squares(L, k)
                        nc.scalar.activation(table_warm[:, 2:3], ones[:, :], ACT.Silu)
                    act.wait_ge(o_turned, DT * L + j + 1)
                    nc.scalar.activation(o_hi[:, j, :], bank[T_BANK[O_T_BANK[j]]][:, :], ACT.Copy,
                                         scale=column("group_gains", DT * L + j)).then_inc(o_hi_ready, 1)
                for j in range(2, OUT_SLABS + 1):
                    split(L, OUT0 + j)
                normal(L, 2)

            act.wait_ge(small_landed, 16)
            nc.scalar.activation(table_warm[:, 1:2], ones[:, :], ACT.Silu)
            for d in range(DT):
                act.wait_ge(x_landed[d // 2], 16)
                normal_tile(0, d)
                if d == 0:
                    act.wait_ge(half_landed, 16)
                    nc.scalar.activation(w_hi[0][:, 0:SLAB // 2], raw[0][:, 0:SLAB // 2], ACT.Copy).then_inc(half_hi, 1)
                if d == 1:
                    act.wait_ge(raw_landed[0], 16)
                    nc.scalar.activation(w_hi[0][:, SLAB // 2:], raw[0][:, SLAB // 2:], ACT.Copy).then_inc(split_hi, 1)
            with act.Fori(0, DEPTH) as L:
                ffn(L, 0)
                mixer(L)
                ffn(L, 1)

        @block.vector
        def _(dve):
            def split_lo_of(s):
                nc.vector.tensor_tensor(w_lo[s][:, :], raw[s][:, :], w_hi[s][:, :].bitcast(F32), ALU.subtract)\
                  .then_inc(split_lo, 1)

            def split(L, j):
                dve.wait_ge(split_hi, LAYER_SLABS * L + j + 1)
                split_lo_of(j % 2)

            def normal_lo(m, d):
                dve.wait_ge(h_hi_ready, DT * m + d + 1)
                nc.vector.scalar_tensor_tensor(h_lo[:, d, :], x[:, d, :], column("gains", DT * m + d),
                                               h_hi[:, d, :].bitcast(F32), ALU.mult, ALU.subtract).then_inc(h_ready, 1)

            def residual(L, part, scale):
                m = instance(L, part)
                for d in range(DT):
                    if (part, d) in RESID_AT:
                        dve.wait_ge(resid_done, len(RESID_AT) * L + RESID_AT[part, d])
                    else:
                        j = {1: FFN_SLABS - 1, 2: OUT0 + (1 if d < 4 else 3), 3: LAYER_SLABS - 1}[part]
                        dve.wait_ge(slab_used, slab_end(L, j))
                    nc.vector.scalar_tensor_tensor(x[:, d, :], bank[DB[d]][:, :], scale, x[:, d, :],
                                                   ALU.mult, ALU.add).then_inc(x_ready, 1)
                    if d:
                        normal_lo(m, d - 1)
                normal_lo(m, DT - 1)

            def token_variance(L, part):
                m = instance(L, part)
                dve.wait_ge(sum_done, m + 1)
                nc.vector.tensor_scalar(var_col[:, :], bank[SUM_BANK][:, 0:TB], 1.0 / D_MODEL, EPS,
                                        ALU.mult, ALU.add).then_inc(var_ready, 1)

            def ffn(L, w):
                base = FFN_BASE[w]
                f0 = 2 * FT * L + FT * w

                def gate(F, s):
                    dve.wait_ge(gate_done, F + 1)
                    nc.vector.tensor_tensor(gs[s][:, :], bank[GATE_BANK[s]][:, :], rstd_row[:, :], ALU.mult)\
                      .then_inc(gate_read, 1)

                def product(j, F, s):
                    dve.wait_ge(slab_used, LAYER_SLABS * L + j + (base + 1 + SLOTS))
                    nc.vector.tensor_tensor(us[s][:, :], bank[UP_BANK[s]][:, :], rstd_row[:, :], ALU.mult)\
                      .then_inc(up_read, 1)
                    dve.wait_ge(silu_done, F + 1)
                    dve.wait_ge(up_read, F + 1)
                    nc.vector.tensor_tensor(us[s][:, :], us[s][:, :], gs[s][:, :], ALU.mult).then_inc(u_ready, 1)

                def split_at(s, j):
                    dve.wait_ge(split_hi, LAYER_SLABS * L + j + (base + 1))
                    split_lo_of(s)

                def hidden_at(i, e):
                    dve.wait_ge(u_hi_ready, f0 + 2 * i + (e + 1))
                    nc.vector.tensor_tensor(u_lo[:, bass.ds(2 * i + e, 1), :],
                                            us[e][:, :].rearrange("p (o c) -> p o c", o=1),
                                            u_hi[:, bass.ds(2 * i + e, 1), :].bitcast(F32),
                                            ALU.subtract).then_inc(u_lo_ready, 1)

                split_at((base + 1) % 2, 1)
                token_variance(L, 2 * w)
                split_at(base % 2, 2)
                dve.wait_ge(row_ready, 2 * L + (w + 1))
                gate(f0, 0)
                product(0, f0, 0)
                hidden_at(0, 0)
                gate(f0 + 1, 1)
                with dve.Fori(1, FT // 2) as i:
                    for e in range(2):
                        product(2 * i + (e - 1), f0 + 2 * i + (e - 1), 1 - e)
                        split_at((base + e + 1) % 2, 2 * i + (e + 1))
                        hidden_at(i - (1 - e), 1 - e)
                        gate(f0 + 2 * i + e, e)
                product(FT - 1, f0 + (FT - 1), 1)
                split_at((base + FT + 1) % 2, FT + 1)
                hidden_at(FT // 2 - 1, 1)
                with dve.Fori(1, DOWN_SLABS // 2) as i:
                    for e in range(2):
                        split_at((base + FT + e) % 2, 2 * i + (FT + e))
                split_at((base + FT) % 2, FT + 2 * (DOWN_SLABS // 2))
                split_at((base + FT + 1) % 2, FT + DOWN_SLABS)
                residual(L, 2 * w + 1, 0.5)

            def tile(L, c, tb):
                t = q = TB * c + tb
                heads = 2 * PAIRS[c]
                width = HEAD_DIM * heads
                X = bank[PROJ_BANKS[t % len(PROJ_BANKS)]]
                s = q % 2
                dve.wait_ge(tile_squared, TILES * L + t + 1)
                if q >= 2:
                    dve.wait_ge(roped, QK_TILES * L + q - 1)
                nc.vector.reduce_sum(head_ss[s][:, 0:heads],
                                     bank[SQ_BANK][:, 0:width].rearrange("p (h f) -> p h f", f=HEAD_DIM),
                                     axis=AX_X).then_inc(heads_summed, 1)
                dve.wait_ge(tables_ready, KINDS * L + (2 * c + 2 if c < 2 else c + 3))
                if q >= TB:
                    dve.wait_ge(group_done, QK_TILES * L + q - TB + 1)
                parts = ((2 * c, 0, 4), (2 * c + 1, 4, 2)) if c < 2 else ((c + 2, 0, heads),)
                axial = c == 0
                for kind, h0, n in parts:
                    final = kind == parts[-1][0]
                    cols = slice(h0 * HEAD_DIM, (h0 + n) * HEAD_DIM)
                    cosines = rope_cos[:, kind, tb:tb + 1, :].broadcast_to([P, n, HEAD_DIM])
                    nc.vector.tensor_tensor(qk_tok[:, tb, cols].rearrange("p (h f) -> p h f", f=HEAD_DIM),
                                            X[:, cols].rearrange("p (h f) -> p h f", f=HEAD_DIM), cosines, ALU.mult)
                    if final:
                        dve.wait_ge(heads_summed, QK_TILES * L + q + 1)
                        nc.vector.scalar_tensor_tensor(head_var[s][:, 0:heads], head_ss[s][:, 0:heads], 1.0 / HEAD_DIM,
                                                       eps_var[:, tb:tb + 1].broadcast_to([P, heads]),
                                                       ALU.mult, ALU.add).then_inc(head_var_ready, 1)
                    for y in range(2):
                        if axial:
                            view, shape = "p (h a y f) -> p y h a f", dict(a=2, y=2, f=HALF // 2)
                            table = rope_sin[:, kind, tb:tb + 1, :].rearrange("p o (a y f) -> p y o a f", **{k: v for k, v in shape.items()})[:, y]\
                                .broadcast_to([P, n, 2, HALF // 2])
                        else:
                            view, shape = "p (h y f) -> p y h f", dict(y=2, f=HALF)
                            table = rope_sin[:, kind, tb:tb + 1, :].rearrange("p o (y f) -> p y o f", y=2)[:, y]\
                                .broadcast_to([P, n, HALF])
                        last = nc.vector.tensor_tensor(gs[s][:, cols].rearrange(view, **shape)[:, y],
                                                       X[:, cols].rearrange(view, **shape)[:, 1 - y], table, ALU.mult)
                last.then_inc(rope_parts, 1)

            def group(L, q):
                c, tb = q // TB, q % TB
                dve.wait_ge(group_hi, QK_TILES * L + q + 1)
                pairs = slice(PAIR0[c], PAIR0[c] + PAIRS[c])
                nc.vector.tensor_tensor(qk_lo[:, pairs, tb * P:(tb + 1) * P],
                                        bank[T_BANK[q % 2]][:, 0:P * PAIRS[c]].rearrange("p (n t) -> p n t", t=P),
                                        qk_hi[:, pairs, tb * P:(tb + 1) * P].bitcast(F32), ALU.subtract)\
                  .then_inc(t_read[q % 2], 1)

            def scores(L, a):
                i, qb, other = unit(a)
                blocks = unit_blocks(a)
                width = P * len(blocks)
                dve.wait_ge(mask_landed, 16)
                dve.wait_ge(s_done, UNITS * L + a + 1)
                if a >= S_RING:
                    dve.wait_ge(p_ready, UNITS * L + a - S_RING + 1)
                nc.vector.sem_inc(scores_begun, 1)
                S = bank[S_BANK[a % S_RING]][:, 0:width]
                dst, low = s_masked[a % S_RING][:, 0:width], neg_max[:, a:a + 1]
                if other and i < B_HEADS:
                    ins = nc.vector.tensor_scalar(dst, S, -SCALE, 3.0e38, ALU.mult, ALU.min, accum_out=low)
                elif other:
                    c0 = P * (blocks[0] - (qb - 1))
                    ins = nc.vector.tensor_tensor_reduce(out=dst, in0=S, in1=mask_c[:, c0:c0 + width], scale=-SCALE,
                                                         scalar=nsink[:, i - B_HEADS:i - B_HEADS + 1],
                                                         op0=ALU.add, op1=ALU.min, accum_out=low)
                else:
                    c0 = P * (TB - 1 - qb)
                    ins = nc.vector.tensor_tensor_reduce(out=dst, in0=S, in1=mask_a[:, c0:c0 + SEQ], scale=-SCALE,
                                                         scalar=3.0e38, op0=ALU.add, op1=ALU.min, accum_out=low)
                ins.then_inc(s_read, 1)

            def finish_head(L, i, other):
                n = head_number(i, other)
                O = bank[O_BANK[n % 2]][:, 0:TB * VW].rearrange("p (b f) -> p b f", f=VW)
                dve.wait_ge(pv_done, UNITS * L + head_units(i, other).stop)
                total = O[:, :, HEAD_DIM]
                if other and i >= B_HEADS:
                    g = i - B_HEADS
                    dve.wait_ge(sink_ready, C_HEADS * L + g + 1)
                    nc.vector.tensor_tensor(den[:, :], total, sink_exp[:, g, :], ALU.add).then_inc(den_ready, 1)
                    dve.wait_ge(den_ready, C_HEADS * L + g + 1)
                    total = den[:, :]
                nc.vector.reciprocal(rden[n % 2][:, :], total).then_inc(rden_ready, 1)
                dve.wait_ge(rden_ready, 16 * L + n + 1)
                c0 = HEAD_DIM * (i if not other else A_HEADS + i)
                nc.vector.tensor_tensor(o_tok[:, :, c0:c0 + HEAD_DIM], O[:, :, 0:HEAD_DIM],
                                        rden[n % 2][:, :].rearrange("p (b o) -> p b o", o=1).broadcast_to([P, TB, HEAD_DIM]),
                                        ALU.mult).then_inc(o_ready, 1)

            def group_variance(L, n):
                dve.wait_ge(squared, len(SQUARES) * L + 2 * TB * (n + 1))
                nc.vector.scalar_tensor_tensor(group_var[:, n, :], group_ss[:, n, 0, :], GROUPS[n][1] * EPS,
                                               group_ss[:, n, 1, :], ALU.add, ALU.add).then_inc(group_var_ready, 1)

            def group_scale(L, n, blocks):
                c0, width, _ = GROUPS[n]
                dve.wait_ge(group_rstd_ready, 3 * L + n + 1)
                for tb in blocks:
                    cols = o_tok[:, tb, c0:c0 + width]
                    nc.vector.tensor_scalar(cols, cols, group_rstd[:, n, tb:tb + 1], math.sqrt(width), ALU.mult, ALU.mult)\
                      .then_inc(o_scaled, 1)

            def output_lo(L, j):
                dve.wait_ge(o_hi_ready, DT * L + j + 1)
                nc.vector.scalar_tensor_tensor(o_lo[:, j, :], bank[T_BANK[O_T_BANK[j]]][:, :],
                                               column("group_gains", DT * L + j), o_hi[:, j, :].bitcast(F32),
                                               ALU.mult, ALU.subtract).then_inc(t_read[O_T_BANK[j]], 1)

            def attention(L):
                for step in range(UNITS + V_LAG + 1):
                    a = step - V_LAG - 1
                    if 0 <= a < UNITS - 1 and unit(a)[1] == TB - 1:
                        finish_head(L, unit(a)[0], unit(a)[2])
                    if step < UNITS:
                        scores(L, step)
                    a = step - T_LAG
                    if 0 <= a < UNITS and not unit(a)[2]:
                        dve.wait_ge(p_used, UNITS * L + a + 1)
                        if a >= 2:
                            dve.wait_ge(pv_done, UNITS * L + a - 1)
                        c0 = P * unit(a)[1]
                        nc.vector.tensor_tensor(probs_t[a % 2][:, :], bank[T_BANK[a % 2]][:, :], count_a[:, c0:c0 + SEQ],
                                                ALU.mult).then_inc(t_read[a % 2], 1)
                    if step in SPLIT_LO_STEPS:
                        j, n = OUT0 + 1, SPLIT_LO_STEPS.index(step)
                        dve.wait_ge(split_hi, LAYER_SLABS * L + j + 1)
                        quarter = slice(n * SLAB // 4, (n + 1) * SLAB // 4)
                        ins = nc.vector.tensor_tensor(w_lo[j % 2][:, quarter], raw[j % 2][:, quarter],
                                                      w_hi[j % 2][:, quarter].bitcast(F32), ALU.subtract)
                        if n == 3:
                            ins.then_inc(split_lo, 1)
                    a = step - V_LAG - 1
                    if a == UNITS - 1:
                        output_lo(L, 0)
                        output_lo(L, 1)
                        finish_head(L, unit(a)[0], unit(a)[2])
                    if step in VARIANCE_STEPS:
                        group_variance(L, VARIANCE_STEPS[step])
                    if step in SCALE_STEPS:
                        group_scale(L, *SCALE_STEPS[step])

            def mixer(L):
                for c in range(CHUNKS):
                    for half in range(2):
                        split(L, PROJ0 + 2 * c + half + 1)
                        if c == 0 and half == 0:
                            token_variance(L, 1)
                            dve.wait_ge(var_ready, instance(L, 1) + 1)
                            nc.vector.tensor_scalar(eps_var[:, :], var_col[:, :], EPS, None, ALU.mult)\
                              .then_inc(eps_var_ready, 1)
                            dve.wait_ge(eps_var_ready, L + 1)
                        for tb in range(TB):
                            if c and (half, tb) in GROUP_AT:
                                group(L, TB * (c - 1) + GROUP_AT.index((half, tb)))
                            if half and c < QK_CHUNKS:
                                tile(L, c, tb)
                attention(L)
                for j in range(DT):
                    if j == TB:
                        group_variance(L, 2)
                        group_scale(L, 2, range(TB))
                    if j > 1:
                        output_lo(L, j)
                for j in range(2, OUT_SLABS + 1):
                    split(L, OUT0 + j)
                residual(L, 2, 1.0)

            dve.wait_ge(small_landed, 16)
            for d in range(DT):
                normal_lo(0, d)
                for half, ready in ((0, half_hi), (1, split_hi)):
                    if d == half:
                        cols = slice(half * SLAB // 2, (half + 1) * SLAB // 2)
                        dve.wait_ge(ready, 1)
                        ins = nc.vector.tensor_tensor(w_lo[0][:, cols], raw[0][:, cols], w_hi[0][:, cols].bitcast(F32),
                                                      ALU.subtract)
                        if half:
                            ins.then_inc(split_lo, 1)
            with dve.Fori(0, DEPTH) as L:
                ffn(L, 0)
                mixer(L)
                ffn(L, 1)

        @block.gpsimd
        def _(pool):
            def sum_squares(m, first):
                for d in range(1, DT):
                    pool.wait_ge(sq_ready, DT * m + d + 1)
                    if d > 1:
                        pool.wait_ge(sq_added, (DT - 1) * m + d - 1)
                    nc.gpsimd.tensor_tensor(square_sum[:, :], square_sum[:, :], gs[d % 2][:, :], ALU.add)\
                      .then_inc(sq_added, 1)

            def token_rstd(m):
                pool.wait_ge(var_ready, m + 1)
                nc.gpsimd.tensor_tensor(rstd_col[:, :], var_col[:, :], nhalf[:, 0:TB], ALU.pow).then_inc(rstd_ready, 1)

            def tables(L, kind):
                axial = kind < 2
                a, f = (2, HALF // 2) if axial else (1, HALF)
                names = ("cosB", "sinB", "nsinB") if axial else ("cosA", "sinA", "nsinA")
                cos, sin, nsin = (small_of(n).rearrange("p (t a f) -> p t a f", t=TB, a=a) for n in names)
                g0 = PACK["head_gains"][0]
                gain = pack[:, bass.ds(KINDS * HEAD_DIM * L + (g0 + kind * HEAD_DIM), HEAD_DIM)]\
                    .rearrange("p (a y f) -> p a y f", a=a, y=2)
                for y in range(2):
                    for dst, wave, src in ((rope_cos, cos, y), (rope_sin, sin if y else nsin, 1 - y)):
                        to = dst[:, kind].rearrange("p t (a y f) -> p t a y f", a=a, y=2)
                        for k in range(a):
                            g = gain[:, k:k + 1, src, :].broadcast_to([P, TB, f])
                            last = nc.gpsimd.tensor_tensor(to[:, :, k, y, :], wave[:, :, k, :], g, ALU.mult)
                last.then_inc(tables_ready, 1)

            def tile(L, q):
                c, tb, s = q // TB, q % TB, q % 2
                heads = 2 * PAIRS[c]
                width = heads * HEAD_DIM
                pool.wait_ge(head_var_ready, QK_TILES * L + q + 1)
                nc.gpsimd.tensor_tensor(head_rstd[s][:, 0:heads], head_var[s][:, 0:heads], nhalf[:, 0:heads], ALU.pow)
                pool.wait_ge(rope_parts, QK_TILES * L + q + 1)
                part = qk_tok[:, tb, 0:width]
                nc.gpsimd.tensor_tensor(part, part, gs[s][:, 0:width], ALU.add).then_inc(rope_sum, 1)
                pool.wait_ge(rope_sum, QK_TILES * L + q + 1)
                part = part.rearrange("p (h f) -> p h f", f=HEAD_DIM)
                factor = head_rstd[s][:, 0:heads].rearrange("p (h o) -> p h o", o=1).broadcast_to([P, heads, HEAD_DIM])
                nc.gpsimd.tensor_tensor(part, part, factor, ALU.mult).then_inc(roped, 1)

            def mixer(L):
                pool.wait_ge(rope_landed, 16)
                pool.wait_ge(slab_used, slab_end(L, FFN_SLABS - 1))
                s0 = PACK["sinks"][0]
                nc.gpsimd.tensor_tensor(nsink[:, :], pack[:, bass.ds(C_HEADS * L + s0, C_HEADS)], small_of("minus"), ALU.mult)\
                  .then_inc(nsink_ready, 1)
                nc.gpsimd.memset(v_tok[:, :, :, HEAD_DIM:VW], 1.0).then_inc(v_ones, 1)
                tables(L, 0)
                token_rstd(instance(L, 1))
                tables(L, 1)
                for q in range(QK_TILES):
                    tile(L, q)
                    if q in TABLES_AFTER:
                        tables(L, TABLES_AFTER[q])
                for n in range(3):
                    pool.wait_ge(group_var_ready, 3 * L + n + 1)
                    nc.gpsimd.tensor_tensor(group_rstd[:, n, :], group_var[:, n, :], nhalf[:, 0:TB], ALU.pow)\
                      .then_inc(group_rstd_ready, 1)

            pool.wait_ge(small_landed, 16)
            sum_squares(0, True)
            with pool.Fori(0, DEPTH) as L:
                token_rstd(instance(L, 0))
                sum_squares(instance(L, 1), False)
                mixer(L)
                sum_squares(instance(L, 2), False)
                token_rstd(instance(L, 2))
                sum_squares(instance(L, 3), False)

        @block.tensor
        def _(pe):
            def three(dst, a_hi, a_lo, b_hi, b_lo, start, stop):
                nc.tensor.matmul(dst, a_hi, b_hi, start=start, stop=False)
                nc.tensor.matmul(dst, a_hi, b_lo, start=False, stop=False)
                return nc.tensor.matmul(dst, a_lo, b_hi, start=False, stop=stop)

            def sum_of_squares(L, part):
                m = instance(L, part)
                pe.wait_ge(sq_added, (DT - 1) * m + (DT - 1))
                for tb in range(TB):
                    last = nc.tensor.matmul(bank[SUM_BANK][:, tb:tb + 1], square_sum[:, tb * P:(tb + 1) * P],
                                            ones[:, :], start=True, stop=True)
                last.then_inc(sum_done, 1)

            def rstd_as_row(L, w):
                pe.wait_ge(rstd_ready, instance(L, 2 * w) + 1)
                for tb in range(TB):
                    last = nc.tensor.matmul(bank[ROW_BANK][:, tb * P:(tb + 1) * P],
                                            rstd_col[:, tb:tb + 1].broadcast_to([P, P]), ident, start=True, stop=True)
                last.then_inc(row_done, 1)

            def ffn(L, w):
                base, m = FFN_BASE[w], instance(L, 2 * w)
                f0 = 2 * FT * L + FT * w

                def gemm(dst, s, c0):
                    for k in range(DT):
                        cols = slice(c0 + k * P, c0 + (k + 1) * P)
                        last = three(dst[:, :], w_hi[s][:, cols], w_lo[s][:, cols], h_hi[:, k, :], h_lo[:, k, :],
                                     k == 0, k == DT - 1)
                    return last

                def up_slab(s, e, j, F, first=None):
                    pe.wait_ge(split_lo, LAYER_SLABS * L + j + (base + 1))
                    pe.wait_ge(gate_read, F + (FREE - 1))
                    if first == 0:
                        for k in range(DT):
                            pe.wait_ge(h_ready, DT * m + k + 1)
                            for dst, c0, done in ((bank[GATE_BANK[e]], 0, gate_done), (bank[UP_BANK[e]], DT * P, slab_used)):
                                cols = slice(c0 + k * P, c0 + (k + 1) * P)
                                last = three(dst[:, :], w_hi[s][:, cols], w_lo[s][:, cols], h_hi[:, k, :], h_lo[:, k, :],
                                             k == 0, k == DT - 1)
                                if k == DT - 1:
                                    last.then_inc(done, 1)
                        sum_of_squares(L, 2 * w)
                        return
                    gemm(bank[GATE_BANK[e]], s, 0).then_inc(gate_done, 1)
                    if first == 1:
                        rstd_as_row(L, w)
                    if first is None:
                        pe.wait_ge(up_read, F - 1)
                    gemm(bank[UP_BANK[e]], s, DT * P).then_inc(slab_used, 1)

                def down_slab(s, j, i, e0, first=False, last=False):
                    pe.wait_ge(split_lo, LAYER_SLABS * L + j + (base + 1))

                    def part(d, e, start, stop):
                        f = bass.ds(2 * i + (2 * e0 + e), 1)
                        cols = slice(e * D_MODEL + d * P, e * D_MODEL + (d + 1) * P)
                        return three(bank[DB[d]][:, :], w_hi[s][:, cols], w_lo[s][:, cols], u_hi[:, f, :], u_lo[:, f, :],
                                     start, stop)

                    if last:
                        pe.wait_ge(u_lo_ready, f0 + FT)
                        for d in range(DT):
                            part(d, 0, False, False)
                            part(d, 1, False, True).then_inc(resid_done if d < DT - 1 else slab_used, 1)
                        return
                    for e in range(2):
                        pe.wait_ge(u_lo_ready, f0 + 2 * i + (2 * e0 + e + 1))
                        for d in (4, 5, 6, 7, 0, 1, 2, 3):
                            if first and e == 0 and d == 0:
                                pe.wait_ge(gate_read, f0 + (FT + FREE))
                                pe.wait_ge(up_read, f0 + FT)
                            ins = part(d, e, first and e == 0, False)
                    ins.then_inc(slab_used, 1)

                up_slab(base % 2, 0, 0, f0, first=0)
                up_slab((base + 1) % 2, 1, 1, f0 + 1, first=1)
                with pe.Fori(1, FT // 2) as i:
                    for e in range(2):
                        up_slab((base + e) % 2, e, 2 * i + e, f0 + 2 * i + e)
                down_slab((base + FT) % 2, FT, 0, 0, first=True)
                with pe.Fori(0, DOWN_SLABS // 2 - 1) as i:
                    down_slab((base + FT + 1) % 2, 2 * i + (FT + 1), 2 * i, 1)
                    down_slab((base + FT) % 2, 2 * i + (FT + 2), 2 * i, 2)
                down_slab((base + FT + 1) % 2, FT + DOWN_SLABS - 2, 0, DOWN_SLABS - 2)
                down_slab((base + FT) % 2, FT + DOWN_SLABS - 1, 0, DOWN_SLABS - 1, last=True)

            def wait_bank(L, key):
                b, n = uses[key]
                if n > 1:
                    pe.wait_ge(t_read[b], T_USES[b] * L + n - 1)
                return bank[T_BANK[b]]

            def wait_copied(L, key):
                b, n = uses[key]
                pe.wait_ge(t_read[b], T_USES[b] * L + n)

            def group(L, q):
                c, tb = q // TB, q % TB
                pe.wait_ge(roped, QK_TILES * L + q + 1)
                dst = wait_bank(L, ("group", q))
                for n in range(PAIRS[c]):
                    last = nc.tensor.transpose(dst[:, n * P:(n + 1) * P], qk_tok[:, tb, n * P:(n + 1) * P], ident)
                last.then_inc(group_done, 1)

            def projection(L):
                m = instance(L, 1)
                for c in range(CHUNKS):
                    for half in range(2):
                        j = PROJ0 + 2 * c + half
                        pe.wait_ge(split_lo, LAYER_SLABS * L + j + 1)
                        for tb in range(TB):
                            t = TB * c + tb
                            if c and (half, tb) in GROUP_AT:
                                group(L, TB * (c - 1) + GROUP_AT.index((half, tb)))
                            if not half:
                                past = t - len(PROJ_BANKS)
                                if past >= 0:
                                    pe.wait_ge(rope_parts, QK_TILES * L + past + 1)
                            for k in range(4):
                                kk = 4 * half + k
                                if c == 0 and tb == 0:
                                    pe.wait_ge(h_ready, DT * m + kk + 1)
                                rows = slice(tb * P, (tb + 1) * P)
                                last = three(bank[PROJ_BANKS[t % len(PROJ_BANKS)]][:, :], h_hi[:, kk, rows], h_lo[:, kk, rows],
                                             w_hi[j % 2][:, k * KW:(k + 1) * KW], w_lo[j % 2][:, k * KW:(k + 1) * KW],
                                             kk == 0, kk == DT - 1)
                            if tb == TB - 1:
                                last.then_inc(slab_used, 1)
                            elif half:
                                last.then_inc(proj_done, 1)
                        if c == 0 and half == 0:
                            sum_of_squares(L, 1)

            def scores(L, a):
                i, qb, other = unit(a)
                if a >= S_RING:
                    pe.wait_ge(s_read, UNITS * L + a - S_RING + 1)
                elif a:
                    pe.wait_ge(tile_squared, TILES * L + QK_TILES + a)
                else:
                    for q in (QK_TILES - 2, QK_TILES - 1):
                        wait_copied(L, ("group", q))
                pq, pk, r, _ = unit_qkv(a)
                rows = slice(r, r + HEAD_DIM)
                blocks = unit_blocks(a)
                keys = slice(P * blocks[0], P * (blocks[-1] + 1))
                queries = slice(P * qb, P * (qb + 1))
                three(bank[S_BANK[a % S_RING]][:, 0:P * len(blocks)], qk_hi[rows, pq, queries], qk_lo[rows, pq, queries],
                      qk_hi[rows, pk, keys], qk_lo[rows, pk, keys], True, True).then_inc(s_done, 1)

            def turn(L, a):
                other = unit(a)[2]
                pe.wait_ge(p_ready, UNITS * L + a + 1)
                dst = wait_bank(L, ("unit", a))
                n = len(unit_blocks(a))
                for b in range(n):
                    at = b if other else n - 1 - b
                    last = nc.tensor.transpose(dst[:, at * P:(at + 1) * P], probs[a % S_RING][:, b * P:(b + 1) * P], ident)
                last.then_inc(p_used, 1)

            def values(L, a):
                i, qb, other = unit(a)
                head = head_number(i, other)
                v = unit_qkv(a)[3]
                wait_copied(L, ("unit", a))
                if a == 0:
                    pe.wait_ge(rope_parts, QK_TILES * (L + 1))
                    pe.wait_ge(tile_squared, TILES * (L + 1))
                    pe.wait_ge(v_ones, L + 1)
                elif qb == 0 and head > 1:
                    pe.wait_ge(o_ready, 16 * L + head - 1)
                blocks = unit_blocks(a)
                for n, kb in enumerate(blocks):
                    at = n if other else len(blocks) - 1 - n
                    last = nc.tensor.matmul(bank[O_BANK[head % 2]][:, qb * VW:(qb + 1) * VW],
                                            probs_t[a % 2][:, at * P:(at + 1) * P], v_tok[:, kb, v, :],
                                            start=n == 0, stop=n == len(blocks) - 1)
                last.then_inc(pv_done, 1)

            def attention(L):
                for step in range(UNITS + V_LAG):
                    if step < UNITS:
                        scores(L, step)
                    if 0 <= step - T_LAG < UNITS:
                        turn(L, step - T_LAG)
                    if step == UNITS + V_LAG - 1:
                        pe.wait_ge(o_scaled, 3 * TB * L + 2 * TB)
                        turn_output(L, 0)
                    if 0 <= step - V_LAG:
                        values(L, step - V_LAG)

            def turn_output(L, *tiles):
                for j in tiles:
                    dst = wait_bank(L, ("o", j))
                    for tb in range(TB):
                        last = nc.tensor.transpose(dst[:, tb * P:(tb + 1) * P], o_tok[:, tb, j * P:(j + 1) * P], ident)
                    last.then_inc(o_turned, 1)

            def output(L):
                turn_output(L, 1)
                pe.wait_ge(o_ready, 16 * L + 15)
                turn_output(L, 2)
                for dh in range(2):
                    for kh in range(2):
                        j = OUT0 + 2 * dh + kh
                        pe.wait_ge(split_lo, LAYER_SLABS * L + j + 1)
                        first = dh == 0 and kh == 0
                        if first:
                            pe.wait_ge(s_read, UNITS * (L + 1))
                        if dh == 0 and kh == 1:
                            for tile in (5, 6, 7):
                                wait_copied(L, ("o", tile))
                        for dd in range(4):
                            if first and dd == 2:
                                turn_output(L, 4, 5)
                            if first and dd == 3:
                                pe.wait_ge(squared, len(SQUARES) * (L + 1))
                                pe.wait_ge(o_scaled, 3 * TB * (L + 1))
                                turn_output(L, 6, 7)
                            for k in range(4):
                                if first and dd == 0:
                                    wait_copied(L, ("o", k))
                                    if k == 0:
                                        turn_output(L, 3)
                                cols = slice(k * KW + dd * P, k * KW + (dd + 1) * P)
                                last = three(bank[DB[4 * dh + dd]][:, :], w_hi[j % 2][:, cols], w_lo[j % 2][:, cols],
                                             o_hi[:, 4 * kh + k, :], o_lo[:, 4 * kh + k, :],
                                             kh == 0 and k == 0, kh == 1 and k == 3)
                            if dd == 3:
                                last.then_inc(slab_used, 1)
                            elif kh:
                                last.then_inc(resid_done, 1)

            nc.tensor.sem_inc(slab_used, SLOTS)
            nc.tensor.sem_inc(gate_read, FREE)
            pe.wait_ge(small_landed, 16)
            with pe.Fori(0, DEPTH) as L:
                ffn(L, 0)
                projection(L)
                attention(L)
                output(L)
                ffn(L, 1)


def _rope_tables(pos, dim):
    inv_freq = (1.0 / (np.float32(ROPE_THETA) ** (np.arange(0, dim, 2, dtype=np.float32) / np.float32(dim)))).astype(np.float32)
    ang = (pos.astype(np.float32)[:, None] * inv_freq[None, :]).astype(np.float32)
    return np.cos(ang.astype(np.float64)).astype(np.float32), np.sin(ang.astype(np.float64)).astype(np.float32)


def _constants():
    t = np.arange(SEQ)
    cos_a, sin_a = _rope_tables(t, HEAD_DIM)
    cos_r, sin_r = _rope_tables(t // GRID_W, HALF)
    cos_c, sin_c = _rope_tables(t % GRID_W, HALF)
    cos_b, sin_b = np.concatenate([cos_r, cos_c], 1), np.concatenate([sin_r, sin_c], 1)

    def by_block(a):
        return a.reshape(TB, P, -1).transpose(1, 0, 2).reshape(P, -1)

    cols = {"ident": np.eye(P), "ones": np.ones((P, 1)), "nhalf": np.full((P, 8), -0.5), "minus": np.full((P, C_HEADS), -1.0),
            "cosA": by_block(cos_a), "sinA": by_block(sin_a), "nsinA": by_block(-sin_a),
            "cosB": by_block(cos_b), "sinB": by_block(sin_b), "nsinB": by_block(-sin_b)}
    rel = np.arange(TOEP_A)[None, :] - (TB - 1) * P - np.arange(P)[:, None]
    count = sum(((rel % dil == 0) & (np.abs(rel) <= (window // (2 * dil)) * dil)).astype(np.float32)
                for window, dil in DILATED_PATTERNS)
    rel_c = np.arange(TOEP_C)[None, :] - P - np.arange(P)[:, None]
    masks = np.concatenate([np.where(count > 0, 0.0, MASK_VALUE), count,
                            np.where(np.abs(rel_c) <= C_RADIUS, 0.0, MASK_VALUE)], 1)
    return {k: v.astype(np.float32) for k, v in cols.items()}, masks


def _slabs(a):
    out = np.empty((N_SLABS + 1, P, SLAB), np.float32)
    q_order = [0, 2, 1, 3]
    cols, at = [], 0
    for heads in (A_HEADS, A_HEADS, A_HEADS, B_HEADS, B_KV_HEADS, B_KV_HEADS, C_HEADS, C_KV_HEADS, C_KV_HEADS):
        c = np.arange(at, at + heads * HEAD_DIM).reshape(heads, HEAD_DIM)
        cols.append((c[q_order] if heads == 4 else c).ravel())
        at += heads * HEAD_DIM
    cols = np.concatenate(cols[3:] + cols[:3])
    n = 0
    for l in range(DEPTH):
        for w in (1, 2):
            if w == 2:
                w_in = a["w_in"][l][:, cols].reshape(2, 4, P, CHUNKS, KW)
                out[n:n + PROJ_SLABS] = w_in.transpose(3, 0, 2, 1, 4).reshape(PROJ_SLABS, P, SLAB)
                n += PROJ_SLABS
                w_out = a["w_out"][l].reshape(2, 4, P, 2, KW)
                out[n:n + OUT_SLABS] = w_out.transpose(3, 0, 2, 1, 4).reshape(OUT_SLABS, P, SLAB)
                n += OUT_SLABS
            both = np.stack([a[f"ffn{w}_w_gate"][l], a[f"ffn{w}_w_up"][l]])
            both = both.reshape(2, DT, P, FT, P)
            out[n:n + FT] = both.transpose(3, 2, 0, 1, 4).reshape(FT, P, SLAB)
            n += FT
            down = a[f"ffn{w}_w_down"][l].reshape(DOWN_SLABS, 2, P, D_MODEL)
            out[n:n + DOWN_SLABS] = down.transpose(0, 2, 1, 3).reshape(DOWN_SLABS, P, SLAB)
            n += DOWN_SLABS
    assert n == N_SLABS
    out[n] = out[0]
    return out


def kernel(**inputs):
    import concourse.bacc as _bacc
    import ml_dtypes as _ml
    from concourse.bass_utils import run_bass_kernel_spmd as _run

    a = {k: np.asarray(v) for k, v in inputs.items()}
    cols, masks = _constants()

    def by_tile(g):
        return g.reshape(-1, DT, P).transpose(2, 0, 1).reshape(P, -1)

    norms = np.stack([a[n][l] for l in range(DEPTH) for n in ("ffn1_norm", "mix_norm", "ffn2_norm")] + [a["ffn1_norm"][0]])
    heads = np.stack([a[n][l] for l in range(DEPTH) for n in
                      ("b_q_norm", "b_k_norm", "c_q_norm", "c_k_norm", "a_q_norm", "a_k_norm")])
    cols["gains"] = by_tile(norms)
    cols["group_gains"] = by_tile(a["group_norm"])
    cols["head_gains"] = np.broadcast_to(heads.reshape(1, -1), (P, heads.size))
    cols["sinks"] = np.broadcast_to(a["c_sink"].reshape(1, -1), (P, a["c_sink"].size))
    arrays = {
        "slabs": _slabs(a),
        "x_in": np.ascontiguousarray(a["x"][0].T.reshape(DT, P, SEQ).transpose(1, 0, 2)),
        "small": np.ascontiguousarray(np.concatenate([cols[k] for k in PACK], 1).astype(np.float32)),
        "masks": masks.astype(_ml.bfloat16),
    }
    nc = _bacc.Bacc("TRN2", target_bir_lowering=False, num_devices=1)
    args = [nc.dram_tensor(k, v.shape, mybir.dt.from_np(v.dtype), kind="ExternalInput").ap() for k, v in arrays.items()]
    out = nc.dram_tensor("out", (P, DT, SEQ), F32, kind="ExternalOutput").ap()
    encoder_trunk(nc, *args, out)
    r = _run(nc, [arrays], core_ids=[0])
    y = r.results[0]["out"]
    return y.transpose(1, 0, 2).reshape(D_MODEL, SEQ).T.reshape(1, SEQ, D_MODEL)
```

```python
import math
from contextlib import ExitStack

import numpy as np

import concourse.bass as bass
from concourse import mybir

ALU = mybir.AluOpType
ACT = mybir.ActivationFunctionType
AX_X = mybir.AxisListType.X
F32 = mybir.dt.float32
F32R = mybir.dt.float32r
BF16 = mybir.dt.bfloat16

P = 128
D_MODEL = 1024
SEQ = 512
DEPTH = 2
HEAD_DIM = 64
HALF = HEAD_DIM // 2
D_FF = 2816
A_HEADS, B_HEADS, C_HEADS = 8, 4, 4
B_KV_HEADS = C_KV_HEADS = 2
GRID_W = 64
C_RADIUS = 128
DILATED_PATTERNS = ((128, 1), (512, 4), (2048, 16))
ROPE_THETA = 10000.0
EPS = 1e-6
MASK_VALUE = -1e30
SCALE = 1.0 / math.sqrt(HEAD_DIM)

TB = SEQ // P
DT = D_MODEL // P
FT = D_FF // P
VW = HEAD_DIM + 1

SLAB = 2048
KW = 512
UP_SLABS = FT
DOWN_SLABS = FT // 2
FFN_SLABS = UP_SLABS + DOWN_SLABS
CHUNKS = 5
PROJ_SLABS = 2 * CHUNKS
OUT_SLABS = 4
LAYER_SLABS = 2 * FFN_SLABS + PROJ_SLABS + OUT_SLABS
PROJ0 = FFN_SLABS
OUT0 = PROJ0 + PROJ_SLABS
FFN_BASE = (0, OUT0 + OUT_SLABS)
N_SLABS = DEPTH * LAYER_SLABS

QK_CHUNKS = 4
TILES = CHUNKS * TB
QK_TILES = QK_CHUNKS * TB
PAIRS = (3, 3, 4, 4)
QUERY_PAIRS = (2, 2, 4, 0)
Q_HEADS = A_HEADS + B_HEADS + C_HEADS
K_HEADS = A_HEADS + B_KV_HEADS + C_KV_HEADS
TOK_SLOTS = 3
X_PIECES = ((0, 1), (1, 2), (2, 4), (4, 6), (6, 8))
LATE_KEYS = 6
V_HEADS = A_HEADS + B_KV_HEADS + C_KV_HEADS
KINDS = 6
TABLES_AFTER = {0: 2, 1: 3, 4: 4, 5: 5}
UNITS = 64
S_RING = 3
T_LAG, V_LAG = 3, 5
SPLIT_HI_STEPS, SPLIT_LO_STEPS = (8, 10, 12, 14), (16, 18, 20, 22)
GROUPS = ((8 * HEAD_DIM, 4 * HEAD_DIM, (2, 2)), (0, 8 * HEAD_DIM, (6, 2)), (12 * HEAD_DIM, 4 * HEAD_DIM, (2, 2)))
SQUARES = [(n, part, tb) for n, part in ((0, 0), (0, 1), (1, 0), (1, 1), (2, 0), (2, 1)) for tb in range(TB)]
SQUARE_STEPS = (28, 31, 34, 37, 44, 45, 46, 47, 49, 51, 53, 55, 61, 61, 62, 62)
VARIANCE_STEPS = {49: 0, 63: 1}
SCALE_STEPS = {51: (0, (0,)), 52: (0, (1,)), 53: (0, (2,)), 54: (0, (3,)), 64: (1, tuple(range(TB)))}
GROUP_AT = ((0, 1), (0, 3), (1, 0), (1, 1))
RESID_AT = {k: n + 1 for n, k in enumerate((part, d) for part in (1, 2, 3) for d in range(DT)
                                           if d < DT - 1 and (part, d) != (2, 3))}

DB = (0, 1, 2, 7, 5, 6, 3, 4)
GATE_BANK, UP_BANK = (0, 2), (1, 7)
SUM_BANK, ROW_BANK = 6, 5
PROJ_BANKS = (0, 1, 2, 7, 5)
SQ_BANK = 6
T_BANK = (3, 4, 5, 6)
O_T_BANK = (0, 1, 2, 0, 1, 2, 0, 1)
S_BANK = (0, 1, 2)
O_BANK = (5, 6)
JUNK_BANK = 7

PACK = {}
_at = 0
for _name, _width in (("ident", P), ("ones", 1), ("nhalf", 8), ("minus", C_HEADS),
                      ("gains", (3 * DEPTH + 1) * DT), ("group_gains", DEPTH * DT), ("sinks", DEPTH * C_HEADS),
                      ("head_gains", DEPTH * KINDS * HEAD_DIM), ("cosA", TB * HALF), ("sinA", TB * HALF),
                      ("nsinA", TB * HALF), ("cosB", TB * HALF), ("sinB", TB * HALF), ("nsinB", TB * HALF)):
    PACK[_name] = (_at, _at + _width)
    _at += _width
PACK_W = _at
TOEP_A = SEQ + (TB - 1) * P
TOEP_C = 3 * P


def steps_at(c, half, tb):
    steps = []
    if c and (half, tb) == (1, 0):
        steps.append(("tok", TB * c - 1))
    if c and (half, tb) in GROUP_AT:
        steps.append(("group", TB * (c - 1) + GROUP_AT.index((half, tb))))
    if tb == (2 if c and not half else 0):
        steps.append(("slab",))
    if half:
        steps.append(("tile",))
    if half and tb >= 2 and c < QK_CHUNKS:
        steps.append(("tok", TB * c + tb - 2))
    if c and (half, tb) == (0, 2):
        steps.append(("tok", TB * c - 2))
    return steps


def c_blocks(qb):
    return range(max(0, qb - 1), min(TB - 1, qb + 1) + 1)


def unit_order():
    units = [(i, qb, 0) for i in range(2) for qb in range(TB)]
    for i in range(6):
        for qb in range(TB):
            units += [(i, qb, 1), (i + 2, qb, 0)]
    return units + [(i, qb, 1) for i in (6, 7) for qb in range(TB)]


UNIT_ORDER = unit_order()
HEADS_ENDING = [(i, other) for i, qb, other in UNIT_ORDER if qb == TB - 1]


def unit(a):
    return UNIT_ORDER[a]


def head_number(i, other):
    return HEADS_ENDING.index((i, other))


def head_units(i, other):
    at = [a for a in range(UNITS) if unit(a)[0] == i and unit(a)[2] == other]
    return slice(at[0], at[-1] + 1, at[1] - at[0])


GROUP_HEADS = ((head_number(1, 1) + 1, head_number(3, 1) + 1), (head_number(5, 0) + 1, head_number(7, 0) + 1),
               (head_number(5, 1) + 1, head_number(7, 1) + 1))


def unit_qkv(a):
    i, _, other = unit(a)
    if not other:
        return i, i, HEAD_DIM * (i % 2)
    g, q, k = (i, A_HEADS, A_HEADS) if i < B_HEADS else (i - B_HEADS, A_HEADS + B_HEADS, A_HEADS + B_KV_HEADS)
    return q + 2 * (g % 2) + g // 2, k + g // 2, HEAD_DIM * (g // 2)


def unit_blocks(a):
    i, qb, other = unit(a)
    return c_blocks(qb) if other and i >= B_HEADS else range(TB)


def group_pieces(c):
    if c < 2:
        q, k = A_HEADS + B_HEADS * c, A_HEADS + B_KV_HEADS * c
        return ((("q", q, (0, 1)),), (("k", k, (2,)), ("k_lo", k // 2, (2,))))
    if c == 2:
        return ((("q", 0, (0, 1)),), (("q", 4, (2, 3)),))
    return ((("k", 0, (0, 1)),), (("k", 4, (2,)), ("k", 6, (3,))), (("k_lo", 0, (0, 1, 2, 3)),))


GROUP_USES = sum(len(group_pieces(q // TB)) for q in range(QK_TILES))


def transpose_bank_uses():
    count, uses = [0, 0, 0, 0], {}

    def use(key, b):
        count[b] += 1
        uses[key] = (b, count[b])

    for q in range(QK_TILES):
        for part in range(len(group_pieces(q // TB))):
            use(("group", q, part), part if part < 2 else 3)
    for step in range(UNITS + V_LAG):
        if 0 <= step - T_LAG < UNITS:
            use(("unit", step - T_LAG), (step - T_LAG) % 2)
    for j in range(DT):
        use(("o", j), O_T_BANK[j])
    return uses, count


def encoder_trunk(nc, slabs, x_in, small, masks, out):
    uses, T_USES = transpose_bank_uses()
    with ExitStack() as ctx:
        def sb(name, shape, dt=F32, on=ctx):
            return on.enter_context(nc.sbuf_tensor(name, shape, dt))

        def sem(name):
            return ctx.enter_context(nc.semaphore(name))

        x = sb("x", [P, DT, SEQ])
        raw = [sb(f"raw{s}", [P, SLAB]) for s in range(2)]
        w_hi = [sb(f"w_hi{s}", [P, SLAB], F32R) for s in range(2)]
        w_lo = [sb(f"w_lo{s}", [P, SLAB], F32R) for s in range(2)]
        gs = [sb(f"gs{s}", [P, SEQ]) for s in range(2)]
        with ExitStack() as later:
            split_tok0 = sb("split_tok0", [P, KW // P, 4, HEAD_DIM], F32R, on=later)
        us = [sb(f"us{s}", [P, SEQ]) for s in range(2)]
        square_sum = us[1]
        pack = sb("pack", [P, PACK_W])
        mask = sb("mask", [P, 2 * TOEP_A + TOEP_C], BF16)
        var_col = sb("var_col", [P, TB])
        rstd_col = sb("rstd_col", [P, TB])
        eps_var = sb("eps_var", [P, TB])
        head_ss = [sb(f"head_ss{s}", [P, 8]) for s in range(2)]
        head_var = [sb(f"head_var{s}", [P, 8]) for s in range(2)]
        head_rstd = [sb(f"head_rstd{s}", [P, 8]) for s in range(2)]
        ident_r = sb("ident_r", [P, P], F32R)
        nsink = sb("nsink", [P, C_HEADS])
        neg_max = sb("neg_max", [P, UNITS])
        table_warm = sb("table_warm", [P, 4])
        sink_exp = sb("sink_exp", [P, C_HEADS, TB])
        den = sb("den", [P, TB])
        rden = [sb(f"rden{s}", [P, TB]) for s in range(2)]
        group_ss = sb("group_ss", [P, 3, 2, TB])
        group_var = sb("group_var", [P, 3, TB])
        group_rstd = sb("group_rstd", [P, 3, TB])
        with ExitStack() as view:
            o_tok = sb("o_tok", [P, TB, D_MODEL], on=view)
            s_masked = [sb(f"s_masked{s}", [P, SEQ], on=view) for s in range(S_RING)]
            probs = [sb(f"probs{s}", [P, SEQ], on=view) for s in range(S_RING)]
            probs_t = [sb(f"probs_t{s}", [P, SEQ], on=view) for s in range(2)]
        h_hi = sb("h_hi", [P, DT, SEQ], F32R)
        h_lo = sb("h_lo", [P, DT, SEQ], F32R)
        with ExitStack() as view:
            u_hi = sb("u_hi", [P, FT, SEQ], F32R, on=view)
            u_lo = sb("u_lo", [P, FT, SEQ], F32R, on=view)
            rstd_row = sb("rstd_row", [P, SEQ], on=view)
        with ExitStack() as view:
            q_both = sb("q_both", [P, Q_HEADS, SEQ], F32R, on=view)
            k_twice = sb("k_twice", [P, K_HEADS - LATE_KEYS, SEQ], F32R, on=view)
            k_lo = sb("k_lo", [P, K_HEADS // 2, SEQ], F32R, on=view)
            with ExitStack() as early:
                k_lo_tok = sb("k_lo_tok", [P, TB, V_HEADS * VW], F32R, on=early)
            v_tok = sb("v_tok", [P, TB, V_HEADS, VW], on=view)
            with ExitStack() as later:
                k_twice_late = sb("k_twice_late", [P, LATE_KEYS, SEQ], F32R, on=later)
            rope_cos = sb("rope_cos", [P, KINDS, TB, HEAD_DIM], on=view)
            rope_sin = sb("rope_sin", [P, KINDS, TB, HEAD_DIM], on=view)
            qk_tok = [sb(f"qk_tok{s}", [P, KW], on=view) for s in range(TOK_SLOTS)]
            split_tok = [split_tok0, sb("split_tok1", [P, KW // P, 4, HEAD_DIM], F32R, on=view)]
        o_hi, o_lo = q_both[:, 0:DT, :], q_both[:, DT:2 * DT, :]
        bank = [ctx.enter_context(nc.psum_tensor(f"bank{b}", [P, 512], F32)) for b in range(8)]

        def small_of(name):
            return pack[:, PACK[name][0]:PACK[name][1]]

        ident = small_of("ident")
        ones = small_of("ones")
        nhalf = small_of("nhalf")
        mask_a, count_a = mask[:, 0:TOEP_A], mask[:, TOEP_A:2 * TOEP_A]
        mask_c = mask[:, 2 * TOEP_A:2 * TOEP_A + TOEP_C]

        def column(name, n):
            return pack[:, bass.ds(n + PACK[name][0], 1)]

        ident_ready = sem("ident_ready")
        small_landed, rope_landed, mask_landed = sem("small_landed"), sem("rope_landed"), sem("mask_landed")
        x_landed = [sem(f"x_landed{i}") for i in range(len(X_PIECES))]
        raw_landed = [sem(f"raw_landed{s}") for s in range(2)]
        half_landed, half_hi = sem("half_landed"), sem("half_hi")
        split_hi, split_lo = sem("split_hi"), sem("split_lo")
        slab_used = sem("slab_used")
        x_ready = sem("x_ready")
        h_hi_ready, h_ready = sem("h_hi_ready"), sem("h_ready")
        sq_ready, sq_added = sem("sq_ready"), sem("sq_added")
        sum_done, var_ready, rstd_ready = sem("sum_done"), sem("var_ready"), sem("rstd_ready")
        row_done, row_ready = sem("row_done"), sem("row_ready")
        gate_done, resid_done = sem("gate_done"), sem("resid_done")
        gate_read, up_read = sem("gate_read"), sem("up_read")
        silu_done, u_ready = sem("silu_done"), sem("u_ready")
        u_hi_ready, u_lo_ready = sem("u_hi_ready"), sem("u_lo_ready")
        eps_var_ready = sem("eps_var_ready")
        tables_ready, v_ones, nsink_ready = sem("tables_ready"), sem("v_ones"), sem("nsink_ready")
        proj_done, tile_squared, rope_parts = sem("proj_done"), sem("tile_squared"), sem("rope_parts")
        head_var_ready = sem("head_var_ready")
        heads_summed, rope_sum, roped = sem("heads_summed"), sem("rope_sum"), sem("roped")
        tok_hi, tok_split = sem("tok_hi"), sem("tok_split")
        bank_turned = sem("bank_turned")
        t_read = [sem(f"t_read{b}") for b in range(4)]
        scores_begun = sem("scores_begun")
        s_done, s_read, p_ready, p_used = sem("s_done"), sem("s_read"), sem("p_ready"), sem("p_used")
        pv_done, sink_ready = sem("pv_done"), sem("sink_ready")
        den_ready, rden_ready, o_ready = sem("den_ready"), sem("rden_ready"), sem("o_ready")
        squared, group_var_ready, group_rstd_ready = sem("squared"), sem("group_var_ready"), sem("group_rstd_ready")
        o_scaled, o_turned, o_hi_ready = sem("o_scaled"), sem("o_turned"), sem("o_hi_ready")
        out_stored = sem("out_stored")
        SLOTS = 2
        FREE = 2

        block = ctx.enter_context(nc.Block())

        def key_low_tok(c, s):
            if c < 2:
                return split_tok[s][:, 3, 0:2, :].rearrange("p h f -> p (h f)")
            return k_lo_tok[:, TB - 2 + s, 0:KW]

        def heads_of(ap):
            return ap.rearrange("p (h f) -> p h f", f=HEAD_DIM)

        def key_high(k):
            return (k_twice_late, k) if k < LATE_KEYS else (k_twice, k - LATE_KEYS)

        def turned_so_far(L, q, part):
            before = sum(len(group_pieces(p // TB)) for p in range(q))
            return GROUP_USES * L + before + part + 1

        def take_piece(copy, L, q, part):
            b, n = uses["group", q, part]
            cols, at, last = slice(P * (q % TB), P * (q % TB + 1)), 0, None
            for kind, first, pairs in group_pieces(q // TB)[part]:
                if kind == "k_lo":
                    tensor, place, tiles = k_lo, first, len(pairs)
                elif kind == "q":
                    tensor, place, tiles = q_both, first, 2 * len(pairs)
                else:
                    (tensor, place), tiles = key_high(first), 2 * len(pairs)
                last = copy(tensor[:, place:place + tiles, cols],
                            bank[T_BANK[b]][:, at:at + P * tiles].rearrange("p (n t) -> p n t", t=P))
                at += P * tiles
            last.then_inc(t_read[b], 1)

        def slab_end(L, j):
            return LAYER_SLABS * L + j + 1 + SLOTS

        def instance(L, m):
            return 3 * L + m

        @block.sync
        def _(sp):
            early = PACK["head_gains"][0]
            sp.dma_start(pack[:, 0:early], small[:, 0:early]).then_inc(small_landed, 16)
            def x_piece(i):
                tiles = slice(*X_PIECES[i])
                sp.dma_start(x[:, tiles, :], x_in[:, tiles, :]).then_inc(x_landed[i], 16)

            x_piece(0)
            half = SLAB // 2
            sp.dma_start(raw[0][:, 0:half], slabs[0, :, 0:half]).then_inc(half_landed, 16)
            sp.dma_start(raw[0][:, half:], slabs[0, :, half:]).then_inc(raw_landed[0], 16)
            for i in range(1, len(X_PIECES)):
                x_piece(i)
            sp.dma_start(raw[1][:, :], slabs[1]).then_inc(raw_landed[1], 16)
            sp.dma_start(pack[:, early:], small[:, early:]).then_inc(rope_landed, 16)
            sp.dma_start(mask[:, :], masks).then_inc(mask_landed, 16)
            with sp.Fori(1, N_SLABS // 2) as i:
                for s in range(2):
                    sp.wait_ge(split_lo, 2 * i + (s - 1))
                    sp.dma_start(raw[s][:, :], slabs[bass.ds(2 * i + s, 1)].rearrange("o p c -> p (o c)"))\
                      .then_inc(raw_landed[s], 16)
            sp.wait_ge(split_lo, N_SLABS - 1)
            sp.dma_start(raw[0][:, :], slabs[N_SLABS]).then_inc(raw_landed[0], 16)
            for d in range(DT):
                sp.wait_ge(x_ready, DT * (3 * DEPTH - 1) + d + 1)
                sp.dma_start(out[:, d, :], x[:, d, :]).then_inc(out_stored, 16)
            sp.wait_ge(out_stored, 16 * DT)

        @block.scalar
        def _(act):
            def split(L, j):
                s = j % 2
                act.wait_ge(raw_landed[s], 16 * (LAYER_SLABS // 2) * L + 16 * (j // 2 + 1))
                act.wait_ge(slab_used, LAYER_SLABS * L + j + 1)
                nc.scalar.activation(w_hi[s][:, :], raw[s][:, :], ACT.Copy).then_inc(split_hi, 1)

            def split_step(L, base, s, j):
                act.wait_ge(raw_landed[s], (LAYER_SLABS * 8) * L + 8 * j + (8 * (base - s) + 16))
                act.wait_ge(slab_used, LAYER_SLABS * L + j + (base + 1))
                nc.scalar.activation(w_hi[s][:, :], raw[s][:, :], ACT.Copy).then_inc(split_hi, 1)

            def normal_hi(m, d):
                nc.scalar.activation(h_hi[:, d, :], x[:, d, :], ACT.Copy, scale=column("gains", DT * m + d))\
                  .then_inc(h_hi_ready, 1)

            def square_tile(m, d):
                if d >= 3:
                    act.wait_ge(sq_added, (DT - 1) * m + (d - 2))
                dst = square_sum if d == 0 else gs[d % 2]
                nc.scalar.activation(dst[:, :], x[:, d, :], ACT.Square).then_inc(sq_ready, 1)

            def normal(L, part):
                m = instance(L, part)
                for d in range(DT):
                    act.wait_ge(x_ready, DT * m + (d + 1 - DT))
                    normal_hi(m, d)
                    square_tile(m, d)

            def ffn(L, w):
                base, m = FFN_BASE[w], instance(L, 2 * w)
                f0 = 2 * FT * L + FT * w

                def silu(F, s):
                    act.wait_ge(gate_read, F + (1 + FREE))
                    nc.scalar.activation(gs[s][:, :], gs[s][:, :], ACT.Silu).then_inc(silu_done, 1)

                def hidden_at(i, e):
                    act.wait_ge(u_ready, f0 + 2 * i + (e + 1))
                    nc.scalar.activation(u_hi[:, bass.ds(2 * i + e, 1), :], us[e % 2][:, :].rearrange("p (o c) -> p o c", o=1),
                                         ACT.Copy).then_inc(u_hi_ready, 1)

                split_step(L, base, (base + 1) % 2, 1)
                split_step(L, base, base % 2, 2)
                act.wait_ge(row_done, 2 * L + (w + 1))
                nc.scalar.activation(rstd_row[:, :], bank[ROW_BANK][:, :], ACT.Copy).then_inc(row_ready, 1)
                silu(f0, 0)
                hidden_at(0, 0)
                silu(f0 + 1, 1)
                with act.Fori(1, FT // 2) as i:
                    for e in range(2):
                        split_step(L, base, (base + e + 1) % 2, 2 * i + (e + 1))
                        hidden_at(i - (1 - e), 1 - e)
                        silu(f0 + 2 * i + e, e)
                split_step(L, base, (base + FT + 1) % 2, FT + 1)
                hidden_at(FT // 2 - 1, 1)
                with act.Fori(1, DOWN_SLABS // 2) as i:
                    for e in range(2):
                        split_step(L, base, (base + FT + e) % 2, 2 * i + (FT + e))
                split_step(L, base, (base + FT) % 2, FT + 2 * (DOWN_SLABS // 2))
                split_step(L, base, (base + FT + 1) % 2, FT + DOWN_SLABS)
                normal(L, 2 * w + 1)

            def tile(L, c, tb):
                t = TB * c + tb
                if tb == TB - 1:
                    act.wait_ge(slab_used, slab_end(L, PROJ0 + 2 * c + 1))
                else:
                    act.wait_ge(proj_done, CHUNKS * (TB - 1) * L + (TB - 1) * c + tb + 1)
                X = bank[PROJ_BANKS[t % len(PROJ_BANKS)]]
                if c == QK_CHUNKS:
                    ins = nc.scalar.activation(v_tok[:, tb, 0:A_HEADS, 0:HEAD_DIM],
                                               X[:, :].rearrange("p (h f) -> p h f", f=HEAD_DIM),
                                               ACT.Copy, scale=rstd_col[:, tb:tb + 1])
                else:
                    width = 2 * HEAD_DIM * PAIRS[c]
                    if c < 2:
                        v = A_HEADS + B_KV_HEADS * c
                        nc.scalar.activation(v_tok[:, tb, v:v + 2, 0:HEAD_DIM],
                                             X[:, width:].rearrange("p (h f) -> p h f", f=HEAD_DIM),
                                             ACT.Copy, scale=rstd_col[:, tb:tb + 1])
                    if t:
                        act.wait_ge(heads_summed, QK_TILES * L + t)
                    ins = nc.scalar.activation(bank[SQ_BANK][:, 0:width], X[:, 0:width], ACT.Square)
                ins.then_inc(tile_squared, 1)

            def tok_high(L, q):
                pairs, s = PAIRS[q // TB], q % 2
                act.wait_ge(roped, QK_TILES * L + q + 1)
                if q >= 2:
                    act.wait_ge(bank_turned, turned_so_far(L, q - 2, len(group_pieces((q - 2) // TB)) - 1))
                tok, queries = qk_tok[q % TOK_SLOTS], QUERY_PAIRS[q // TB]
                if queries:
                    ins = nc.scalar.activation(split_tok[s][:, 0:queries, 0:4:3, :],
                                               tok[:, 0:P * queries].rearrange("p (n e f) -> p n e f", e=2, f=HEAD_DIM),
                                               ACT.Copy)
                if pairs > queries:
                    keys = heads_of(tok[:, P * queries:P * pairs]).rearrange("p h (o f) -> p h o f", o=1)
                    ins = nc.scalar.activation(split_tok[s][:, queries:pairs, :, :].rearrange("p n (e o) f -> p (n e) o f", o=2),
                                               keys.broadcast_to([P, 2 * (pairs - queries), 2, HEAD_DIM]), ACT.Copy)
                ins.then_inc(tok_hi, 1)

            def group(L, q):
                for part in range(len(group_pieces(q // TB))):
                    b, n = uses["group", q, part]
                    if b != 1:
                        act.wait_ge(bank_turned, turned_so_far(L, q, part))
                        if q == QK_TILES - TB and part == 0:
                            act.wait_ge(rope_parts, QK_TILES * (L + 1))
                        take_piece(lambda to, src: nc.scalar.activation(to, src, ACT.Copy), L, q, part)

            def squares(L, k):
                n, part, tb = SQUARES[k]
                c0, _, heads = GROUPS[n]
                c0, width = c0 + HEAD_DIM * heads[0] * part, HEAD_DIM * heads[part]
                if tb == 0:
                    act.wait_ge(o_ready, 16 * L + GROUP_HEADS[n][part])
                if k:
                    act.wait_ge(squared, len(SQUARES) * L + k)
                nc.scalar.activation(bank[JUNK_BANK][:, 0:width], o_tok[:, tb, c0:c0 + width], ACT.Square,
                                     accum_out=group_ss[:, n, part, tb:tb + 1]).then_inc(squared, 1)

            def attention(L):
                for step in range(UNITS + V_LAG):
                    a = step
                    if a < UNITS:
                        i, qb, other = unit(a)
                        width = P * len(unit_blocks(a))
                        act.wait_ge(s_read, UNITS * L + a + 1)
                        if a >= S_RING:
                            act.wait_ge(p_used, UNITS * L + a - S_RING + 1)
                        nc.scalar.activation(probs[a % S_RING][:, 0:width], s_masked[a % S_RING][:, 0:width], ACT.Exp,
                                             bias=neg_max[:, a:a + 1], scale=-1.0).then_inc(p_ready, 1)
                        if other and i >= B_HEADS and qb == TB - 1:
                            g = i - B_HEADS
                            nc.scalar.activation(sink_exp[:, g, :], neg_max[:, head_units(i, other)], ACT.Exp,
                                                 bias=column("sinks", C_HEADS * L + g)).then_inc(sink_ready, 1)
                    a = step - T_LAG
                    if 0 <= a < UNITS and unit(a)[2]:
                        act.wait_ge(p_used, UNITS * L + a + 1)
                        if a >= 2:
                            act.wait_ge(pv_done, UNITS * L + a - 1)
                        width = P * len(unit_blocks(a))
                        nc.scalar.activation(probs_t[a % 2][:, 0:width], bank[T_BANK[a % 2]][:, 0:width], ACT.Copy)\
                          .then_inc(t_read[a % 2], 1)
                    if step in SPLIT_HI_STEPS:
                        j, n = OUT0 + 1, SPLIT_HI_STEPS.index(step)
                        act.wait_ge(raw_landed[j % 2], 8 * LAYER_SLABS * L + 16 * (j // 2 + 1))
                        act.wait_ge(slab_used, LAYER_SLABS * L + j + 1)
                        quarter = slice(n * SLAB // 4, (n + 1) * SLAB // 4)
                        ins = nc.scalar.activation(w_hi[j % 2][:, quarter], raw[j % 2][:, quarter], ACT.Copy)
                        if n == 3:
                            ins.then_inc(split_hi, 1)
                    for k, at in enumerate(SQUARE_STEPS):
                        if at == step:
                            squares(L, k)

            def mixer(L):
                for c in range(CHUNKS):
                    for half in range(2):
                        for tb in range(TB):
                            if (c, half, tb) == (CHUNKS - 1, 1, TB - 2):
                                nc.scalar.activation(table_warm[:, 0:1], ones[:, :], ACT.Exp)
                            for what, *q in steps_at(c, half, tb):
                                if what == "tok":
                                    tok_high(L, *q)
                                elif what == "group":
                                    group(L, *q)
                                elif what == "slab":
                                    split(L, PROJ0 + 2 * c + half + 1)
                                else:
                                    if (c, tb) == (0, 0):
                                        act.wait_ge(rstd_ready, instance(L, 1) + 1)
                                    tile(L, c, tb)
                attention(L)
                for j in range(DT):
                    if j == TB:
                        for k in range(len(SQUARE_STEPS), len(SQUARES)):
                            squares(L, k)
                        nc.scalar.activation(table_warm[:, 2:3], ones[:, :], ACT.Silu)
                    act.wait_ge(o_turned, DT * L + j + 1)
                    nc.scalar.activation(o_hi[:, j, :], bank[T_BANK[O_T_BANK[j]]][:, :], ACT.Copy,
                                         scale=column("group_gains", DT * L + j)).then_inc(o_hi_ready, 1)
                for j in range(2, OUT_SLABS + 1):
                    split(L, OUT0 + j)
                normal(L, 2)

            act.wait_ge(small_landed, 16)
            nc.scalar.activation(table_warm[:, 1:2], ones[:, :], ACT.Silu)
            for d in range(DT):
                for i, (first, _) in enumerate(X_PIECES):
                    if d == first:
                        act.wait_ge(x_landed[i], 16)
                normal_hi(0, d)
                if d == 0:
                    act.wait_ge(half_landed, 16)
                    nc.scalar.activation(w_hi[0][:, 0:SLAB // 2], raw[0][:, 0:SLAB // 2], ACT.Copy).then_inc(half_hi, 1)
                square_tile(0, d)
                if d == 0:
                    act.wait_ge(raw_landed[0], 16)
                    nc.scalar.activation(w_hi[0][:, SLAB // 2:], raw[0][:, SLAB // 2:], ACT.Copy).then_inc(split_hi, 1)
            with act.Fori(0, DEPTH) as L:
                ffn(L, 0)
                mixer(L)
                ffn(L, 1)

        @block.vector
        def _(dve):
            def split_lo_of(s):
                nc.vector.tensor_tensor(w_lo[s][:, :], raw[s][:, :], w_hi[s][:, :].bitcast(F32), ALU.subtract)\
                  .then_inc(split_lo, 1)

            def split(L, j):
                dve.wait_ge(split_hi, LAYER_SLABS * L + j + 1)
                split_lo_of(j % 2)

            def normal_lo(m, d):
                dve.wait_ge(h_hi_ready, DT * m + d + 1)
                nc.vector.scalar_tensor_tensor(h_lo[:, d, :], x[:, d, :], column("gains", DT * m + d),
                                               h_hi[:, d, :].bitcast(F32), ALU.mult, ALU.subtract).then_inc(h_ready, 1)

            def residual(L, part, scale):
                m = instance(L, part)
                for d in range(DT):
                    if (part, d) in RESID_AT:
                        dve.wait_ge(resid_done, len(RESID_AT) * L + RESID_AT[part, d])
                    else:
                        j = {1: FFN_SLABS - 1, 2: OUT0 + (1 if d < 4 else 3), 3: LAYER_SLABS - 1}[part]
                        dve.wait_ge(slab_used, slab_end(L, j))
                    nc.vector.scalar_tensor_tensor(x[:, d, :], bank[DB[d]][:, :], scale, x[:, d, :],
                                                   ALU.mult, ALU.add).then_inc(x_ready, 1)
                    if d:
                        normal_lo(m, d - 1)
                normal_lo(m, DT - 1)

            def token_variance(L, part):
                m = instance(L, part)
                dve.wait_ge(sum_done, m + 1)
                nc.vector.tensor_scalar(var_col[:, :], bank[SUM_BANK][:, 0:TB], 1.0 / D_MODEL, EPS,
                                        ALU.mult, ALU.add).then_inc(var_ready, 1)

            def ffn(L, w):
                base = FFN_BASE[w]
                f0 = 2 * FT * L + FT * w

                def gate(F, s):
                    dve.wait_ge(gate_done, F + 1)
                    nc.vector.tensor_tensor(gs[s][:, :], bank[GATE_BANK[s]][:, :], rstd_row[:, :], ALU.mult)\
                      .then_inc(gate_read, 1)

                def product(j, F, s):
                    dve.wait_ge(slab_used, LAYER_SLABS * L + j + (base + 1 + SLOTS))
                    nc.vector.tensor_tensor(us[s][:, :], bank[UP_BANK[s]][:, :], rstd_row[:, :], ALU.mult)\
                      .then_inc(up_read, 1)
                    dve.wait_ge(silu_done, F + 1)
                    dve.wait_ge(up_read, F + 1)
                    nc.vector.tensor_tensor(us[s][:, :], us[s][:, :], gs[s][:, :], ALU.mult).then_inc(u_ready, 1)

                def split_at(s, j):
                    dve.wait_ge(split_hi, LAYER_SLABS * L + j + (base + 1))
                    split_lo_of(s)

                def hidden_at(i, e):
                    dve.wait_ge(u_hi_ready, f0 + 2 * i + (e + 1))
                    nc.vector.tensor_tensor(u_lo[:, bass.ds(2 * i + e, 1), :],
                                            us[e][:, :].rearrange("p (o c) -> p o c", o=1),
                                            u_hi[:, bass.ds(2 * i + e, 1), :].bitcast(F32),
                                            ALU.subtract).then_inc(u_lo_ready, 1)

                split_at((base + 1) % 2, 1)
                token_variance(L, 2 * w)
                split_at(base % 2, 2)
                dve.wait_ge(row_ready, 2 * L + (w + 1))
                gate(f0, 0)
                product(0, f0, 0)
                hidden_at(0, 0)
                gate(f0 + 1, 1)
                with dve.Fori(1, FT // 2) as i:
                    for e in range(2):
                        product(2 * i + (e - 1), f0 + 2 * i + (e - 1), 1 - e)
                        split_at((base + e + 1) % 2, 2 * i + (e + 1))
                        hidden_at(i - (1 - e), 1 - e)
                        gate(f0 + 2 * i + e, e)
                product(FT - 1, f0 + (FT - 1), 1)
                split_at((base + FT + 1) % 2, FT + 1)
                hidden_at(FT // 2 - 1, 1)
                with dve.Fori(1, DOWN_SLABS // 2) as i:
                    for e in range(2):
                        split_at((base + FT + e) % 2, 2 * i + (FT + e))
                split_at((base + FT) % 2, FT + 2 * (DOWN_SLABS // 2))
                split_at((base + FT + 1) % 2, FT + DOWN_SLABS)
                residual(L, 2 * w + 1, 0.5)

            def tile_sums(L, c, tb):
                q, heads = TB * c + tb, 2 * PAIRS[c]
                dve.wait_ge(tile_squared, TILES * L + q + 1)
                if q >= 2:
                    dve.wait_ge(head_var_ready, QK_TILES * L + q - 1)
                nc.vector.reduce_sum(head_ss[q % 2][:, 0:heads],
                                     bank[SQ_BANK][:, 0:HEAD_DIM * heads].rearrange("p (h f) -> p h f", f=HEAD_DIM),
                                     axis=AX_X).then_inc(heads_summed, 1)

            def tile(L, c, tb):
                t = q = TB * c + tb
                heads = 2 * PAIRS[c]
                X = bank[PROJ_BANKS[t % len(PROJ_BANKS)]]
                s = q % 2
                if q >= 2:
                    dve.wait_ge(roped, QK_TILES * L + q - 1)
                dve.wait_ge(tables_ready, KINDS * L + (2 * c + 2 if c < 2 else c + 3))
                if q >= TOK_SLOTS:
                    dve.wait_ge(tok_split, QK_TILES * L + q - TOK_SLOTS + 1)
                parts = ((2 * c, 0, 4), (2 * c + 1, 4, 2)) if c < 2 else ((c + 2, 0, heads),)
                axial = c == 0
                for kind, h0, n in parts:
                    final = kind == parts[-1][0]
                    cols = slice(h0 * HEAD_DIM, (h0 + n) * HEAD_DIM)
                    cosines = rope_cos[:, kind, tb:tb + 1, :].broadcast_to([P, n, HEAD_DIM])
                    nc.vector.tensor_tensor(qk_tok[q % TOK_SLOTS][:, cols].rearrange("p (h f) -> p h f", f=HEAD_DIM),
                                            X[:, cols].rearrange("p (h f) -> p h f", f=HEAD_DIM), cosines, ALU.mult)
                    if final:
                        dve.wait_ge(heads_summed, QK_TILES * L + q + 1)
                        nc.vector.scalar_tensor_tensor(head_var[s][:, 0:heads], head_ss[s][:, 0:heads], 1.0 / HEAD_DIM,
                                                       eps_var[:, tb:tb + 1].broadcast_to([P, heads]),
                                                       ALU.mult, ALU.add).then_inc(head_var_ready, 1)
                    for y in range(2):
                        if axial:
                            view, shape = "p (h a y f) -> p y h a f", dict(a=2, y=2, f=HALF // 2)
                            table = rope_sin[:, kind, tb:tb + 1, :].rearrange("p o (a y f) -> p y o a f", **{k: v for k, v in shape.items()})[:, y]\
                                .broadcast_to([P, n, 2, HALF // 2])
                        else:
                            view, shape = "p (h y f) -> p y h f", dict(y=2, f=HALF)
                            table = rope_sin[:, kind, tb:tb + 1, :].rearrange("p o (y f) -> p y o f", y=2)[:, y]\
                                .broadcast_to([P, n, HALF])
                        last = nc.vector.tensor_tensor(gs[s][:, cols].rearrange(view, **shape)[:, y],
                                                       X[:, cols].rearrange(view, **shape)[:, 1 - y], table, ALU.mult)
                last.then_inc(rope_parts, 1)

            def tok_low(L, q):
                pairs, s = PAIRS[q // TB], q % 2
                dve.wait_ge(tok_hi, QK_TILES * L + q + 1)
                tok, queries = qk_tok[q % TOK_SLOTS], QUERY_PAIRS[q // TB]
                if queries:
                    ins = nc.vector.tensor_tensor(split_tok[s][:, 0:queries, 1:3, :],
                                                  tok[:, 0:P * queries].rearrange("p (n e f) -> p n e f", e=2, f=HEAD_DIM),
                                                  split_tok[s][:, 0:queries, 0:4:3, :].bitcast(F32), ALU.subtract)
                if pairs > queries:
                    high = split_tok[s][:, queries:pairs, 0:4:2, :].rearrange("p n e f -> p (n e) f").bitcast(F32)
                    ins = nc.vector.tensor_tensor(heads_of(key_low_tok(q // TB, s)), heads_of(tok[:, P * queries:P * pairs]),
                                                  high, ALU.subtract)
                ins.then_inc(tok_split, 1)

            def group(L, q):
                for part in range(len(group_pieces(q // TB))):
                    if uses["group", q, part][0] == 1:
                        dve.wait_ge(bank_turned, turned_so_far(L, q, part))
                        take_piece(nc.vector.tensor_copy, L, q, part)

            def scores(L, a):
                i, qb, other = unit(a)
                blocks = unit_blocks(a)
                width = P * len(blocks)
                dve.wait_ge(mask_landed, 16)
                dve.wait_ge(s_done, UNITS * L + a + 1)
                if a >= S_RING:
                    dve.wait_ge(p_ready, UNITS * L + a - S_RING + 1)
                nc.vector.sem_inc(scores_begun, 1)
                S = bank[S_BANK[a % S_RING]][:, 0:width]
                dst, low = s_masked[a % S_RING][:, 0:width], neg_max[:, a:a + 1]
                if other and i < B_HEADS:
                    ins = nc.vector.tensor_scalar(dst, S, -SCALE, 3.0e38, ALU.mult, ALU.min, accum_out=low)
                elif other:
                    c0 = P * (blocks[0] - (qb - 1))
                    ins = nc.vector.tensor_tensor_reduce(out=dst, in0=S, in1=mask_c[:, c0:c0 + width], scale=-SCALE,
                                                         scalar=nsink[:, i - B_HEADS:i - B_HEADS + 1],
                                                         op0=ALU.add, op1=ALU.min, accum_out=low)
                else:
                    c0 = P * (TB - 1 - qb)
                    ins = nc.vector.tensor_tensor_reduce(out=dst, in0=S, in1=mask_a[:, c0:c0 + SEQ], scale=-SCALE,
                                                         scalar=3.0e38, op0=ALU.add, op1=ALU.min, accum_out=low)
                ins.then_inc(s_read, 1)

            def finish_head(L, i, other):
                n = head_number(i, other)
                O = bank[O_BANK[n % 2]][:, 0:TB * VW].rearrange("p (b f) -> p b f", f=VW)
                dve.wait_ge(pv_done, UNITS * L + head_units(i, other).stop)
                total = O[:, :, HEAD_DIM]
                if other and i >= B_HEADS:
                    g = i - B_HEADS
                    dve.wait_ge(sink_ready, C_HEADS * L + g + 1)
                    nc.vector.tensor_tensor(den[:, :], total, sink_exp[:, g, :], ALU.add).then_inc(den_ready, 1)
                    dve.wait_ge(den_ready, C_HEADS * L + g + 1)
                    total = den[:, :]
                nc.vector.reciprocal(rden[n % 2][:, :], total).then_inc(rden_ready, 1)
                dve.wait_ge(rden_ready, 16 * L + n + 1)
                c0 = HEAD_DIM * (i if not other else A_HEADS + i)
                nc.vector.tensor_tensor(o_tok[:, :, c0:c0 + HEAD_DIM], O[:, :, 0:HEAD_DIM],
                                        rden[n % 2][:, :].rearrange("p (b o) -> p b o", o=1).broadcast_to([P, TB, HEAD_DIM]),
                                        ALU.mult).then_inc(o_ready, 1)

            def group_variance(L, n):
                dve.wait_ge(squared, len(SQUARES) * L + 2 * TB * (n + 1))
                nc.vector.scalar_tensor_tensor(group_var[:, n, :], group_ss[:, n, 0, :], GROUPS[n][1] * EPS,
                                               group_ss[:, n, 1, :], ALU.add, ALU.add).then_inc(group_var_ready, 1)

            def group_scale(L, n, blocks):
                c0, width, _ = GROUPS[n]
                dve.wait_ge(group_rstd_ready, 3 * L + n + 1)
                for tb in blocks:
                    cols = o_tok[:, tb, c0:c0 + width]
                    nc.vector.tensor_scalar(cols, cols, group_rstd[:, n, tb:tb + 1], math.sqrt(width), ALU.mult, ALU.mult)\
                      .then_inc(o_scaled, 1)

            def output_lo(L, j):
                dve.wait_ge(o_hi_ready, DT * L + j + 1)
                nc.vector.scalar_tensor_tensor(o_lo[:, j, :], bank[T_BANK[O_T_BANK[j]]][:, :],
                                               column("group_gains", DT * L + j), o_hi[:, j, :].bitcast(F32),
                                               ALU.mult, ALU.subtract).then_inc(t_read[O_T_BANK[j]], 1)

            def attention(L):
                for step in range(UNITS + V_LAG + 1):
                    a = step - V_LAG - 1
                    if 0 <= a < UNITS - 1 and unit(a)[1] == TB - 1:
                        finish_head(L, unit(a)[0], unit(a)[2])
                    if step < UNITS:
                        scores(L, step)
                    a = step - T_LAG
                    if 0 <= a < UNITS and not unit(a)[2]:
                        dve.wait_ge(p_used, UNITS * L + a + 1)
                        if a >= 2:
                            dve.wait_ge(pv_done, UNITS * L + a - 1)
                        c0 = P * unit(a)[1]
                        nc.vector.tensor_tensor(probs_t[a % 2][:, :], bank[T_BANK[a % 2]][:, :], count_a[:, c0:c0 + SEQ],
                                                ALU.mult).then_inc(t_read[a % 2], 1)
                    if step in SPLIT_LO_STEPS:
                        j, n = OUT0 + 1, SPLIT_LO_STEPS.index(step)
                        dve.wait_ge(split_hi, LAYER_SLABS * L + j + 1)
                        quarter = slice(n * SLAB // 4, (n + 1) * SLAB // 4)
                        ins = nc.vector.tensor_tensor(w_lo[j % 2][:, quarter], raw[j % 2][:, quarter],
                                                      w_hi[j % 2][:, quarter].bitcast(F32), ALU.subtract)
                        if n == 3:
                            ins.then_inc(split_lo, 1)
                    a = step - V_LAG - 1
                    if a == UNITS - 1:
                        output_lo(L, 0)
                        output_lo(L, 1)
                        finish_head(L, unit(a)[0], unit(a)[2])
                    if step in VARIANCE_STEPS:
                        group_variance(L, VARIANCE_STEPS[step])
                    if step in SCALE_STEPS:
                        group_scale(L, *SCALE_STEPS[step])

            def mixer(L):
                for c in range(CHUNKS):
                    for half in range(2):
                        for tb in range(TB):
                            for what, *q in steps_at(c, half, tb):
                                if what == "tok":
                                    tok_low(L, *q)
                                elif what == "group":
                                    group(L, *q)
                                elif what == "slab":
                                    split(L, PROJ0 + 2 * c + half + 1)
                                elif c < QK_CHUNKS:
                                    tile_sums(L, c, tb)
                                    tile(L, c, tb)
                        if c == 0 and half == 0:
                            token_variance(L, 1)
                            dve.wait_ge(var_ready, instance(L, 1) + 1)
                            nc.vector.tensor_scalar(eps_var[:, :], var_col[:, :], EPS, None, ALU.mult)\
                              .then_inc(eps_var_ready, 1)
                            dve.wait_ge(eps_var_ready, L + 1)
                attention(L)
                for j in range(DT):
                    if j == TB:
                        group_variance(L, 2)
                        group_scale(L, 2, range(TB))
                    if j > 1:
                        output_lo(L, j)
                for j in range(2, OUT_SLABS + 1):
                    split(L, OUT0 + j)
                residual(L, 2, 1.0)

            dve.wait_ge(small_landed, 16)
            nc.vector.tensor_copy(ident_r[:, :], ident).then_inc(ident_ready, 1)
            for d in range(DT):
                normal_lo(0, d)
                if d == 0:
                    for half, ready in ((0, half_hi), (1, split_hi)):
                        cols = slice(half * SLAB // 2, (half + 1) * SLAB // 2)
                        dve.wait_ge(ready, 1)
                        ins = nc.vector.tensor_tensor(w_lo[0][:, cols], raw[0][:, cols], w_hi[0][:, cols].bitcast(F32),
                                                      ALU.subtract)
                        if half:
                            ins.then_inc(split_lo, 1)
            with dve.Fori(0, DEPTH) as L:
                ffn(L, 0)
                mixer(L)
                ffn(L, 1)

        @block.gpsimd
        def _(pool):
            def sum_squares(m, first):
                for d in range(1, DT):
                    pool.wait_ge(sq_ready, DT * m + d + 1)
                    if d > 1:
                        pool.wait_ge(sq_added, (DT - 1) * m + d - 1)
                    nc.gpsimd.tensor_tensor(square_sum[:, :], square_sum[:, :], gs[d % 2][:, :], ALU.add)\
                      .then_inc(sq_added, 1)

            def token_rstd(m):
                pool.wait_ge(var_ready, m + 1)
                nc.gpsimd.tensor_tensor(rstd_col[:, :], var_col[:, :], nhalf[:, 0:TB], ALU.pow).then_inc(rstd_ready, 1)

            def tables(L, kind):
                axial = kind < 2
                a, f = (2, HALF // 2) if axial else (1, HALF)
                names = ("cosB", "sinB", "nsinB") if axial else ("cosA", "sinA", "nsinA")
                cos, sin, nsin = (small_of(n).rearrange("p (t a f) -> p t a f", t=TB, a=a) for n in names)
                g0 = PACK["head_gains"][0]
                gain = pack[:, bass.ds(KINDS * HEAD_DIM * L + (g0 + kind * HEAD_DIM), HEAD_DIM)]\
                    .rearrange("p (a y f) -> p a y f", a=a, y=2)
                for y in range(2):
                    for dst, wave, src in ((rope_cos, cos, y), (rope_sin, sin if y else nsin, 1 - y)):
                        to = dst[:, kind].rearrange("p t (a y f) -> p t a y f", a=a, y=2)
                        for k in range(a):
                            g = gain[:, k:k + 1, src, :].broadcast_to([P, TB, f])
                            last = nc.gpsimd.tensor_tensor(to[:, :, k, y, :], wave[:, :, k, :], g, ALU.mult)
                last.then_inc(tables_ready, 1)

            def tile(L, q):
                c, tb, s = q // TB, q % TB, q % 2
                heads = 2 * PAIRS[c]
                width = heads * HEAD_DIM
                pool.wait_ge(head_var_ready, QK_TILES * L + q + 1)
                nc.gpsimd.tensor_tensor(head_rstd[s][:, 0:heads], head_var[s][:, 0:heads], nhalf[:, 0:heads], ALU.pow)
                pool.wait_ge(rope_parts, QK_TILES * L + q + 1)
                part = qk_tok[q % TOK_SLOTS][:, 0:width]
                nc.gpsimd.tensor_tensor(part, part, gs[s][:, 0:width], ALU.add).then_inc(rope_sum, 1)
                pool.wait_ge(rope_sum, QK_TILES * L + q + 1)
                part = part.rearrange("p (h f) -> p h f", f=HEAD_DIM)
                factor = head_rstd[s][:, 0:heads].rearrange("p (h o) -> p h o", o=1).broadcast_to([P, heads, HEAD_DIM])
                nc.gpsimd.tensor_tensor(part, part, factor, ALU.mult).then_inc(roped, 1)

            def mixer(L):
                pool.wait_ge(rope_landed, 16)
                pool.wait_ge(slab_used, slab_end(L, FFN_SLABS - 1))
                s0 = PACK["sinks"][0]
                nc.gpsimd.tensor_tensor(nsink[:, :], pack[:, bass.ds(C_HEADS * L + s0, C_HEADS)], small_of("minus"), ALU.mult)\
                  .then_inc(nsink_ready, 1)
                tables(L, 0)
                token_rstd(instance(L, 1))
                tables(L, 1)
                for q in range(QK_TILES):
                    tile(L, q)
                    if q in TABLES_AFTER:
                        tables(L, TABLES_AFTER[q])
                pool.wait_ge(bank_turned, GROUP_USES * (L + 1))
                many_ones = ones.rearrange("p (a b c) -> p a b c", a=1, b=1).broadcast_to([P, TB, V_HEADS, 1])
                nc.gpsimd.tensor_tensor(v_tok[:, :, :, HEAD_DIM:VW], many_ones, many_ones, ALU.mult).then_inc(v_ones, 1)
                for n in range(3):
                    pool.wait_ge(group_var_ready, 3 * L + n + 1)
                    nc.gpsimd.tensor_tensor(group_rstd[:, n, :], group_var[:, n, :], nhalf[:, 0:TB], ALU.pow)\
                      .then_inc(group_rstd_ready, 1)

            pool.wait_ge(small_landed, 16)
            sum_squares(0, True)
            with pool.Fori(0, DEPTH) as L:
                token_rstd(instance(L, 0))
                sum_squares(instance(L, 1), False)
                mixer(L)
                sum_squares(instance(L, 2), False)
                token_rstd(instance(L, 2))
                sum_squares(instance(L, 3), False)

        @block.tensor
        def _(pe):
            def three(dst, a_hi, a_lo, b_hi, b_lo, start, stop):
                nc.tensor.matmul(dst, a_hi, b_hi, start=start, stop=False)
                nc.tensor.matmul(dst, a_hi, b_lo, start=False, stop=False)
                return nc.tensor.matmul(dst, a_lo, b_hi, start=False, stop=stop)

            def sum_of_squares(L, part):
                m = instance(L, part)
                pe.wait_ge(sq_added, (DT - 1) * m + (DT - 1))
                for tb in range(TB):
                    last = nc.tensor.matmul(bank[SUM_BANK][:, tb:tb + 1], square_sum[:, tb * P:(tb + 1) * P],
                                            ones[:, :], start=True, stop=True)
                last.then_inc(sum_done, 1)

            def rstd_as_row(L, w):
                pe.wait_ge(rstd_ready, instance(L, 2 * w) + 1)
                for tb in range(TB):
                    last = nc.tensor.matmul(bank[ROW_BANK][:, tb * P:(tb + 1) * P],
                                            rstd_col[:, tb:tb + 1].broadcast_to([P, P]), ident, start=True, stop=True)
                last.then_inc(row_done, 1)

            def ffn(L, w):
                base, m = FFN_BASE[w], instance(L, 2 * w)
                f0 = 2 * FT * L + FT * w

                def gemm(dst, s, c0):
                    for k in range(DT):
                        cols = slice(c0 + k * P, c0 + (k + 1) * P)
                        last = three(dst[:, :], w_hi[s][:, cols], w_lo[s][:, cols], h_hi[:, k, :], h_lo[:, k, :],
                                     k == 0, k == DT - 1)
                    return last

                def up_slab(s, e, j, F, first=None):
                    pe.wait_ge(split_lo, LAYER_SLABS * L + j + (base + 1))
                    pe.wait_ge(gate_read, F + (FREE - 1))
                    if first == 0:
                        for k in range(DT):
                            pe.wait_ge(h_ready, DT * m + k + 1)
                            for dst, c0, done in ((bank[GATE_BANK[e]], 0, gate_done), (bank[UP_BANK[e]], DT * P, slab_used)):
                                cols = slice(c0 + k * P, c0 + (k + 1) * P)
                                last = three(dst[:, :], w_hi[s][:, cols], w_lo[s][:, cols], h_hi[:, k, :], h_lo[:, k, :],
                                             k == 0, k == DT - 1)
                                if k == DT - 1:
                                    last.then_inc(done, 1)
                        sum_of_squares(L, 2 * w)
                        return
                    gemm(bank[GATE_BANK[e]], s, 0).then_inc(gate_done, 1)
                    if first == 1:
                        rstd_as_row(L, w)
                    if first is None:
                        pe.wait_ge(up_read, F - 1)
                    gemm(bank[UP_BANK[e]], s, DT * P).then_inc(slab_used, 1)

                def down_slab(s, j, i, e0, first=False, last=False):
                    pe.wait_ge(split_lo, LAYER_SLABS * L + j + (base + 1))

                    def part(d, e, start, stop):
                        f = bass.ds(2 * i + (2 * e0 + e), 1)
                        cols = slice(e * D_MODEL + d * P, e * D_MODEL + (d + 1) * P)
                        return three(bank[DB[d]][:, :], w_hi[s][:, cols], w_lo[s][:, cols], u_hi[:, f, :], u_lo[:, f, :],
                                     start, stop)

                    if last:
                        pe.wait_ge(u_lo_ready, f0 + FT)
                        for d in range(DT):
                            part(d, 0, False, False)
                            part(d, 1, False, True).then_inc(resid_done if d < DT - 1 else slab_used, 1)
                        return
                    for e in range(2):
                        pe.wait_ge(u_lo_ready, f0 + 2 * i + (2 * e0 + e + 1))
                        for d in (4, 5, 6, 7, 0, 1, 2, 3):
                            if first and e == 0 and d == 0:
                                pe.wait_ge(gate_read, f0 + (FT + FREE))
                                pe.wait_ge(up_read, f0 + FT)
                            ins = part(d, e, first and e == 0, False)
                    ins.then_inc(slab_used, 1)

                up_slab(base % 2, 0, 0, f0, first=0)
                up_slab((base + 1) % 2, 1, 1, f0 + 1, first=1)
                with pe.Fori(1, FT // 2) as i:
                    for e in range(2):
                        up_slab((base + e) % 2, e, 2 * i + e, f0 + 2 * i + e)
                down_slab((base + FT) % 2, FT, 0, 0, first=True)
                with pe.Fori(0, DOWN_SLABS // 2 - 1) as i:
                    down_slab((base + FT + 1) % 2, 2 * i + (FT + 1), 2 * i, 1)
                    down_slab((base + FT) % 2, 2 * i + (FT + 2), 2 * i, 2)
                down_slab((base + FT + 1) % 2, FT + DOWN_SLABS - 2, 0, DOWN_SLABS - 2)
                down_slab((base + FT) % 2, FT + DOWN_SLABS - 1, 0, DOWN_SLABS - 1, last=True)

            def wait_bank(L, key):
                b, n = uses[key]
                if n > 1:
                    pe.wait_ge(t_read[b], T_USES[b] * L + n - 1)
                return bank[T_BANK[b]]

            def wait_copied(L, key):
                b, n = uses[key]
                pe.wait_ge(t_read[b], T_USES[b] * L + n)

            def group(L, q):
                pe.wait_ge(tok_split, QK_TILES * L + q + 1)
                src, parts = split_tok[q % 2], group_pieces(q // TB)
                for part, pieces in enumerate(parts):
                    if part == 2 and q == QK_TILES - TB:
                        pe.wait_ge(heads_summed, QK_TILES * (L + 1))
                    dst, at = wait_bank(L, ("group", q, part))[:, :].bitcast(F32R), 0
                    for kind, _, pairs in pieces:
                        for n in pairs:
                            if kind != "k_lo":
                                turns = tuple(src[:, n, e:e + 2, :].rearrange("p h f -> p (h f)") for e in (0, 2))
                            else:
                                first = P * (n - QUERY_PAIRS[q // TB])
                                turns = (key_low_tok(q // TB, q % 2)[:, first:first + P],)
                            for turn_in in turns:
                                last = nc.tensor.transpose(dst[:, at:at + P], turn_in, ident_r[:, :])
                                at += P
                    last.then_inc(bank_turned, 1)

            def projection(L):
                m = instance(L, 1)
                for c in range(CHUNKS):
                    for half in range(2):
                        j = PROJ0 + 2 * c + half
                        pe.wait_ge(split_lo, LAYER_SLABS * L + j + 1)
                        for tb in range(TB):
                            t = TB * c + tb
                            if c and (half, tb) in GROUP_AT:
                                group(L, TB * (c - 1) + GROUP_AT.index((half, tb)))
                            if not half:
                                past = t - len(PROJ_BANKS)
                                if past >= 0:
                                    pe.wait_ge(rope_parts, QK_TILES * L + past + 1)
                            for k in range(4):
                                kk = 4 * half + k
                                if c == 0 and tb == 0:
                                    pe.wait_ge(h_ready, DT * m + kk + 1)
                                rows = slice(tb * P, (tb + 1) * P)
                                last = three(bank[PROJ_BANKS[t % len(PROJ_BANKS)]][:, :], h_hi[:, kk, rows], h_lo[:, kk, rows],
                                             w_hi[j % 2][:, k * KW:(k + 1) * KW], w_lo[j % 2][:, k * KW:(k + 1) * KW],
                                             kk == 0, kk == DT - 1)
                            if tb == TB - 1:
                                last.then_inc(slab_used, 1)
                            elif half:
                                last.then_inc(proj_done, 1)
                        if c == 0 and half == 0:
                            sum_of_squares(L, 1)

            def scores(L, a):
                i, qb, other = unit(a)
                if a >= S_RING:
                    pe.wait_ge(s_read, UNITS * L + a - S_RING + 1)
                elif a:
                    pe.wait_ge(tile_squared, TILES * L + QK_TILES + a)
                else:
                    for part in range(3):
                        wait_copied(L, ("group", QK_TILES - 1, part))
                q, k, r = unit_qkv(a)
                rows = slice(r, r + HEAD_DIM)
                high, place = key_high(k)
                blocks = unit_blocks(a)
                keys = slice(P * blocks[0], P * (blocks[-1] + 1))
                queries = slice(P * qb, P * (qb + 1))
                S = bank[S_BANK[a % S_RING]][:, 0:P * len(blocks)]
                nc.tensor.matmul(S, q_both[:, q, queries], high[:, place, keys], start=True, stop=False)
                nc.tensor.matmul(S, q_both[rows, q, queries], k_lo[rows, k // 2, keys], start=False, stop=True)\
                  .then_inc(s_done, 1)

            def turn(L, a):
                other = unit(a)[2]
                pe.wait_ge(p_ready, UNITS * L + a + 1)
                dst = wait_bank(L, ("unit", a))
                n = len(unit_blocks(a))
                for b in range(n):
                    at = b if other else n - 1 - b
                    last = nc.tensor.transpose(dst[:, at * P:(at + 1) * P], probs[a % S_RING][:, b * P:(b + 1) * P], ident)
                last.then_inc(p_used, 1)

            def values(L, a):
                i, qb, other = unit(a)
                head = head_number(i, other)
                v = unit_qkv(a)[1]
                wait_copied(L, ("unit", a))
                if a == 0:
                    pe.wait_ge(rope_parts, QK_TILES * (L + 1))
                    pe.wait_ge(tile_squared, TILES * (L + 1))
                    pe.wait_ge(v_ones, L + 1)
                elif qb == 0 and head > 1:
                    pe.wait_ge(o_ready, 16 * L + head - 1)
                blocks = unit_blocks(a)
                for n, kb in enumerate(blocks):
                    at = n if other else len(blocks) - 1 - n
                    last = nc.tensor.matmul(bank[O_BANK[head % 2]][:, qb * VW:(qb + 1) * VW],
                                            probs_t[a % 2][:, at * P:(at + 1) * P], v_tok[:, kb, v, :],
                                            start=n == 0, stop=n == len(blocks) - 1)
                last.then_inc(pv_done, 1)

            def attention(L):
                for step in range(UNITS + V_LAG):
                    if step < UNITS:
                        scores(L, step)
                    if 0 <= step - T_LAG < UNITS:
                        turn(L, step - T_LAG)
                    if step == UNITS + V_LAG - 1:
                        pe.wait_ge(o_scaled, 3 * TB * L + 2 * TB)
                        turn_output(L, 0)
                    if 0 <= step - V_LAG:
                        values(L, step - V_LAG)

            def turn_output(L, *tiles):
                for j in tiles:
                    dst = wait_bank(L, ("o", j))
                    for tb in range(TB):
                        last = nc.tensor.transpose(dst[:, tb * P:(tb + 1) * P], o_tok[:, tb, j * P:(j + 1) * P], ident)
                    last.then_inc(o_turned, 1)

            def output(L):
                turn_output(L, 1)
                pe.wait_ge(o_ready, 16 * L + 15)
                turn_output(L, 2)
                for dh in range(2):
                    for kh in range(2):
                        j = OUT0 + 2 * dh + kh
                        pe.wait_ge(split_lo, LAYER_SLABS * L + j + 1)
                        first = dh == 0 and kh == 0
                        if first:
                            pe.wait_ge(s_read, UNITS * (L + 1))
                        if dh == 0 and kh == 1:
                            for tile in (5, 6, 7):
                                wait_copied(L, ("o", tile))
                        for dd in range(4):
                            if first and dd == 2:
                                turn_output(L, 4, 5)
                            if first and dd == 3:
                                pe.wait_ge(squared, len(SQUARES) * (L + 1))
                                pe.wait_ge(o_scaled, 3 * TB * (L + 1))
                                turn_output(L, 6, 7)
                            for k in range(4):
                                if first and dd == 0:
                                    wait_copied(L, ("o", k))
                                    if k == 0:
                                        turn_output(L, 3)
                                cols = slice(k * KW + dd * P, k * KW + (dd + 1) * P)
                                last = three(bank[DB[4 * dh + dd]][:, :], w_hi[j % 2][:, cols], w_lo[j % 2][:, cols],
                                             o_hi[:, 4 * kh + k, :], o_lo[:, 4 * kh + k, :],
                                             kh == 0 and k == 0, kh == 1 and k == 3)
                            if dd == 3:
                                last.then_inc(slab_used, 1)
                            elif kh:
                                last.then_inc(resid_done, 1)

            nc.tensor.sem_inc(slab_used, SLOTS)
            nc.tensor.sem_inc(gate_read, FREE)
            pe.wait_ge(small_landed, 16)
            with pe.Fori(0, DEPTH) as L:
                ffn(L, 0)
                projection(L)
                attention(L)
                output(L)
                ffn(L, 1)


def _rope_tables(pos, dim):
    inv_freq = (1.0 / (np.float32(ROPE_THETA) ** (np.arange(0, dim, 2, dtype=np.float32) / np.float32(dim)))).astype(np.float32)
    ang = (pos.astype(np.float32)[:, None] * inv_freq[None, :]).astype(np.float32)
    return np.cos(ang.astype(np.float64)).astype(np.float32), np.sin(ang.astype(np.float64)).astype(np.float32)


def _constants():
    t = np.arange(SEQ)
    cos_a, sin_a = _rope_tables(t, HEAD_DIM)
    cos_r, sin_r = _rope_tables(t // GRID_W, HALF)
    cos_c, sin_c = _rope_tables(t % GRID_W, HALF)
    cos_b, sin_b = np.concatenate([cos_r, cos_c], 1), np.concatenate([sin_r, sin_c], 1)

    def by_block(a):
        return a.reshape(TB, P, -1).transpose(1, 0, 2).reshape(P, -1)

    cols = {"ident": np.eye(P), "ones": np.ones((P, 1)), "nhalf": np.full((P, 8), -0.5), "minus": np.full((P, C_HEADS), -1.0),
            "cosA": by_block(cos_a), "sinA": by_block(sin_a), "nsinA": by_block(-sin_a),
            "cosB": by_block(cos_b), "sinB": by_block(sin_b), "nsinB": by_block(-sin_b)}
    rel = np.arange(TOEP_A)[None, :] - (TB - 1) * P - np.arange(P)[:, None]
    count = sum(((rel % dil == 0) & (np.abs(rel) <= (window // (2 * dil)) * dil)).astype(np.float32)
                for window, dil in DILATED_PATTERNS)
    rel_c = np.arange(TOEP_C)[None, :] - P - np.arange(P)[:, None]
    masks = np.concatenate([np.where(count > 0, 0.0, MASK_VALUE), count,
                            np.where(np.abs(rel_c) <= C_RADIUS, 0.0, MASK_VALUE)], 1)
    return {k: v.astype(np.float32) for k, v in cols.items()}, masks


def _slabs(a):
    out = np.empty((N_SLABS + 1, P, SLAB), np.float32)
    q_order = [0, 2, 1, 3]
    cols, at = [], 0
    for heads in (A_HEADS, A_HEADS, A_HEADS, B_HEADS, B_KV_HEADS, B_KV_HEADS, C_HEADS, C_KV_HEADS, C_KV_HEADS):
        c = np.arange(at, at + heads * HEAD_DIM).reshape(heads, HEAD_DIM)
        cols.append((c[q_order] if heads == 4 else c).ravel())
        at += heads * HEAD_DIM
    cols = np.concatenate(cols[3:] + cols[:3])
    n = 0
    for l in range(DEPTH):
        for w in (1, 2):
            if w == 2:
                w_in = a["w_in"][l][:, cols].reshape(2, 4, P, CHUNKS, KW)
                out[n:n + PROJ_SLABS] = w_in.transpose(3, 0, 2, 1, 4).reshape(PROJ_SLABS, P, SLAB)
                n += PROJ_SLABS
                w_out = a["w_out"][l].reshape(2, 4, P, 2, KW)
                out[n:n + OUT_SLABS] = w_out.transpose(3, 0, 2, 1, 4).reshape(OUT_SLABS, P, SLAB)
                n += OUT_SLABS
            both = np.stack([a[f"ffn{w}_w_gate"][l], a[f"ffn{w}_w_up"][l]])
            both = both.reshape(2, DT, P, FT, P)
            out[n:n + FT] = both.transpose(3, 2, 0, 1, 4).reshape(FT, P, SLAB)
            n += FT
            down = a[f"ffn{w}_w_down"][l].reshape(DOWN_SLABS, 2, P, D_MODEL)
            out[n:n + DOWN_SLABS] = down.transpose(0, 2, 1, 3).reshape(DOWN_SLABS, P, SLAB)
            n += DOWN_SLABS
    assert n == N_SLABS
    out[n] = out[0]
    return out


def kernel(**inputs):
    import concourse.bacc as _bacc
    import ml_dtypes as _ml
    from concourse.bass_utils import run_bass_kernel_spmd as _run

    a = {k: np.asarray(v) for k, v in inputs.items()}
    cols, masks = _constants()

    def by_tile(g):
        return g.reshape(-1, DT, P).transpose(2, 0, 1).reshape(P, -1)

    norms = np.stack([a[n][l] for l in range(DEPTH) for n in ("ffn1_norm", "mix_norm", "ffn2_norm")] + [a["ffn1_norm"][0]])
    heads = np.stack([a[n][l] for l in range(DEPTH) for n in
                      ("b_q_norm", "b_k_norm", "c_q_norm", "c_k_norm", "a_q_norm", "a_k_norm")])
    cols["gains"] = by_tile(norms)
    cols["group_gains"] = by_tile(a["group_norm"])
    cols["head_gains"] = np.broadcast_to(heads.reshape(1, -1), (P, heads.size))
    cols["sinks"] = np.broadcast_to(a["c_sink"].reshape(1, -1), (P, a["c_sink"].size))
    arrays = {
        "slabs": _slabs(a),
        "x_in": np.ascontiguousarray(a["x"][0].T.reshape(DT, P, SEQ).transpose(1, 0, 2)),
        "small": np.ascontiguousarray(np.concatenate([cols[k] for k in PACK], 1).astype(np.float32)),
        "masks": masks.astype(_ml.bfloat16),
    }
    nc = _bacc.Bacc("TRN2", target_bir_lowering=False, num_devices=1)
    args = [nc.dram_tensor(k, v.shape, mybir.dt.from_np(v.dtype), kind="ExternalInput").ap() for k, v in arrays.items()]
    out = nc.dram_tensor("out", (P, DT, SEQ), F32, kind="ExternalOutput").ap()
    encoder_trunk(nc, *args, out)
    r = _run(nc, [arrays], core_ids=[0])
    y = r.results[0]["out"]
    return y.transpose(1, 0, 2).reshape(D_MODEL, SEQ).T.reshape(1, SEQ, D_MODEL)
```
